# Optimizing a Trainium2 kernel written in Bass

```python
import jax, jax.numpy as jnp
from jax import lax
import numpy as np

D_MODEL = 1024
BATCH = 1
SEQ = 2048
DEPTH = 1

CHUNK = 64
D_MIX = D_MODEL
ATTN_WIDTH = D_MIX // 2
HEAD_DIM = 64
N_HEADS = ATTN_WIDTH // HEAD_DIM
N_KV_HEADS = 2
GQA_GROUP = N_HEADS // N_KV_HEADS
WINDOW = 128
WINDOW_CHUNKS = WINDOW // CHUNK
ROPE_THETA = 500000.0
ROPE_DIM = HEAD_DIM // 4
POOL_WIDTH = D_MIX - ATTN_WIDTH
POOL_WINDOWS = (2, 4, 8, 16)
POOL_GROUP = POOL_WIDTH // len(POOL_WINDOWS)
KV_WIDTH = N_KV_HEADS * HEAD_DIM
IN_COLS = ATTN_WIDTH + 2 * KV_WIDTH + POOL_WIDTH
N_EXPERTS = 128
EXPERT_DIM = 256
TOP_K = 8
N_EXPERT_GROUPS = 8
TOPK_GROUPS = 4
ROUTED_SCALE = 2.5
SHARED_DIM = EXPERT_DIM
EXPERT_BLOCK = 128
EPS = 1e-6
N_MOD = 6

kernel_name = "hybrid_swa_sink_pool_moe_adaln_block"

def rmsnorm(x, g):
    xf = x.astype(jnp.float32)
    y = xf * lax.rsqrt(jnp.mean(xf * xf, axis=-1, keepdims=True) + EPS)
    return (y * g.astype(jnp.float32)).astype(x.dtype)

def modulate(h, shift, scale):
    return h * (1 + scale[:, None, :]) + shift[:, None, :]

def partial_rope(t, pos):
    half = ROPE_DIM // 2
    inv = jnp.power(ROPE_THETA, -jnp.arange(half, dtype=jnp.float32) * 2.0 / ROPE_DIM)
    ang = pos.astype(jnp.float32)[..., None] * inv
    cos = jnp.cos(ang)[:, :, None, :]
    sin = jnp.sin(ang)[:, :, None, :]
    t1, t2, rest = t[..., :half], t[..., half:ROPE_DIM], t[..., ROPE_DIM:]
    return jnp.concatenate([t1 * cos - t2 * sin, t2 * cos + t1 * sin, rest], axis=-1)

def sink_window_attention(q, k, v, sinks):
    B, S = q.shape[0], q.shape[1]
    NC = S // CHUNK
    qb = q.reshape(B, NC, CHUNK, N_KV_HEADS, GQA_GROUP, HEAD_DIM)

    def band(t):
        t = t.reshape(B, NC, CHUNK, N_KV_HEADS, HEAD_DIM)
        tp = jnp.pad(t, ((0, 0), (WINDOW_CHUNKS - 1, 0), (0, 0), (0, 0), (0, 0)))
        return jnp.concatenate([tp[:, j:j + NC] for j in range(WINDOW_CHUNKS)], axis=2)

    kb, vb = band(k), band(v)
    s = jnp.einsum('bnqkgd,bnskd->bnkgqs', qb, kb) * (HEAD_DIM ** -0.5)
    key_chunk = (jnp.arange(NC)[:, None] - (WINDOW_CHUNKS - 1)
                 + (jnp.arange(WINDOW_CHUNKS * CHUNK) // CHUNK)[None, :])
    valid = key_chunk >= 0
    s = jnp.where(valid[None, :, None, None, None, :], s, -jnp.inf)
    sink = sinks.astype(jnp.float32).reshape(N_KV_HEADS, GQA_GROUP)[None, None, :, :, None, None]
    m = jnp.maximum(s.max(axis=-1, keepdims=True), sink)
    p = jnp.exp(s - m)
    denom = p.sum(axis=-1, keepdims=True) + jnp.exp(sink - m)
    o = jnp.einsum('bnkgqs,bnskd->bnqkgd', p / denom, vb)
    return o.reshape(B, S, N_HEADS * HEAD_DIM)

def multiscale_pool(u, pool_w, pool_scale):
    uf = u.astype(jnp.float32)
    B, S, _ = uf.shape
    csum0 = jnp.pad(jnp.cumsum(uf, axis=1), ((0, 0), (1, 0), (0, 0)))
    t = jnp.arange(S)
    outs = []
    for gi, w in enumerate(POOL_WINDOWS):
        lo, hi = gi * POOL_GROUP, (gi + 1) * POOL_GROUP
        upper = csum0[:, 1:, lo:hi]
        lower = csum0[:, jnp.maximum(t + 1 - w, 0), lo:hi]
        cnt = jnp.minimum(t + 1, w).astype(jnp.float32)[None, :, None]
        outs.append((upper - lower) / cnt - uf[:, :, lo:hi])
    mixed = jnp.stack(outs, axis=2)
    y = jnp.einsum('bsgc,gcd->bsgd', mixed, pool_w.astype(jnp.float32)).reshape(B, S, POOL_WIDTH)
    return (y * pool_scale.astype(jnp.float32)).astype(u.dtype)

def swiglu(h, wg, wu, wd):
    return (jax.nn.silu(h @ wg) * (h @ wu)) @ wd

def moe_ffn(h, w_router, router_bias, w_gate_e, w_up_e, w_down_e, w_sh_gate, w_sh_up, w_sh_down):
    B, S, D = h.shape
    T = B * S
    hf = h.reshape(T, D)
    scores = jax.nn.sigmoid(hf.astype(jnp.float32) @ w_router.astype(jnp.float32))
    choice = scores + router_bias.astype(jnp.float32)[None, :]
    grp = choice.reshape(T, N_EXPERT_GROUPS, N_EXPERTS // N_EXPERT_GROUPS)
    grp_score = lax.top_k(grp, 2)[0].sum(axis=-1)
    _, gidx = lax.top_k(grp_score, TOPK_GROUPS)
    gmask = jax.nn.one_hot(gidx, N_EXPERT_GROUPS, dtype=jnp.float32).sum(axis=1) > 0
    emask = jnp.repeat(gmask, N_EXPERTS // N_EXPERT_GROUPS, axis=1)
    _, eidx = lax.top_k(jnp.where(emask, choice, -jnp.inf), TOP_K)
    wts = jnp.take_along_axis(scores, eidx, axis=1)
    wts = wts / wts.sum(axis=-1, keepdims=True) * ROUTED_SCALE

    TK = T * TOP_K
    R = TK + N_EXPERTS * EXPERT_BLOCK
    NB = R // EXPERT_BLOCK
    flat_e = eidx.reshape(TK)
    flat_tok = jnp.repeat(jnp.arange(T, dtype=jnp.int32), TOP_K)
    flat_w = wts.reshape(TK)
    order = jnp.argsort(flat_e, stable=True)
    se, stok, sw = flat_e[order], flat_tok[order], flat_w[order]
    counts = jnp.bincount(flat_e, length=N_EXPERTS)
    starts = jnp.cumsum(counts) - counts
    padded = (counts + EXPERT_BLOCK - 1) // EXPERT_BLOCK * EXPERT_BLOCK
    pends = jnp.cumsum(padded)
    pstarts = pends - padded
    dest = pstarts[se] + (jnp.arange(TK) - starts[se])
    row_tok = jnp.full((R,), T, dtype=jnp.int32).at[dest].set(stok)
    row_w = jnp.zeros((R,), jnp.float32).at[dest].set(sw)
    block_e = jnp.clip(jnp.searchsorted(pends, jnp.arange(NB) * EXPERT_BLOCK, side='right'),
                       0, N_EXPERTS - 1)
    hp = jnp.concatenate([hf, jnp.zeros((1, D), hf.dtype)], axis=0)

    def expert_block(args):
        tok, rw, e = args
        xs = hp[tok]
        y = swiglu(xs, w_gate_e[e], w_up_e[e], w_down_e[e])
        return (y.astype(jnp.float32) * rw[:, None]).astype(hf.dtype)

    y = lax.map(expert_block, (row_tok.reshape(NB, EXPERT_BLOCK),
                               row_w.reshape(NB, EXPERT_BLOCK), block_e))
    routed = jnp.zeros((T + 1, D), hf.dtype).at[row_tok].add(y.reshape(R, D))[:T]
    shared = swiglu(hf, w_sh_gate, w_sh_up, w_sh_down)
    return (routed + shared).reshape(B, S, D)

def hybrid_layer(x, c, positions, ada_w, ada_b, norm1_g, w_in, attn_sinks, pool_w, pool_scale,
                 w_out, norm2_g, w_router, router_bias, w_gate_e, w_up_e, w_down_e,
                 w_sh_gate, w_sh_up, w_sh_down):
    B, S, D = x.shape
    mod = jax.nn.silu(c) @ ada_w + ada_b
    shift1, scale1, gate1, shift2, scale2, gate2 = jnp.split(mod, N_MOD, axis=-1)

    h = modulate(rmsnorm(x, norm1_g), shift1, scale1)
    proj = h @ w_in
    q = proj[..., :ATTN_WIDTH]
    k = proj[..., ATTN_WIDTH:ATTN_WIDTH + KV_WIDTH]
    v = proj[..., ATTN_WIDTH + KV_WIDTH:ATTN_WIDTH + 2 * KV_WIDTH]
    u = proj[..., ATTN_WIDTH + 2 * KV_WIDTH:]
    q = partial_rope(q.reshape(B, S, N_HEADS, HEAD_DIM).astype(jnp.float32), positions)
    k = partial_rope(k.reshape(B, S, N_KV_HEADS, HEAD_DIM).astype(jnp.float32), positions)
    v = v.reshape(B, S, N_KV_HEADS, HEAD_DIM).astype(jnp.float32)
    a = sink_window_attention(q, k, v, attn_sinks).astype(x.dtype)
    p = multiscale_pool(u, pool_w, pool_scale)
    mix = jnp.concatenate([a, p], axis=-1) @ w_out
    x = x + gate1[:, None, :] * mix

    h2 = modulate(rmsnorm(x, norm2_g), shift2, scale2)
    f = moe_ffn(h2, w_router, router_bias, w_gate_e, w_up_e, w_down_e, w_sh_gate, w_sh_up, w_sh_down)
    return x + gate2[:, None, :] * f

def setup_inputs(seed: int = 0) -> dict:
    key = jax.random.key(seed)
    ks = jax.random.split(key, 24)
    nrm = lambda k, shape, s: jax.random.normal(k, shape, jnp.float32) * s
    L, D, E, F = DEPTH, D_MODEL, N_EXPERTS, EXPERT_DIM
    x = nrm(ks[0], (BATCH, SEQ, D), 1.0)
    c = nrm(ks[1], (BATCH, D), 1.0)
    offs = jax.random.randint(ks[2], (BATCH, 1), 0, 4096, dtype=jnp.int32)
    positions = (offs + jnp.arange(SEQ, dtype=jnp.int32)[None, :]).astype(jnp.int32)
    return {
        "x": x,
        "c": c,
        "positions": positions,
        "ada_w": nrm(ks[3], (L, D, N_MOD * D), 0.5 * D ** -0.5),
        "ada_b": nrm(ks[4], (L, N_MOD * D), 0.02),
        "norm1_g": 1.0 + nrm(ks[5], (L, D), 0.02),
        "w_in": nrm(ks[6], (L, D, IN_COLS), D ** -0.5),
        "attn_sinks": nrm(ks[7], (L, N_HEADS), 0.5),
        "pool_w": nrm(ks[8], (L, len(POOL_WINDOWS), POOL_GROUP, POOL_GROUP), POOL_GROUP ** -0.5),
        "pool_scale": 1.0 + nrm(ks[9], (L, POOL_WIDTH), 0.1),
        "w_out": nrm(ks[10], (L, D_MIX, D), D_MIX ** -0.5),
        "norm2_g": 1.0 + nrm(ks[11], (L, D), 0.02),
        "w_router": nrm(ks[12], (L, D, E), D ** -0.5),
        "router_bias": nrm(ks[13], (L, E), 0.01),
        "w_gate_e": nrm(ks[14], (L, E, D, F), D ** -0.5),
        "w_up_e": nrm(ks[15], (L, E, D, F), D ** -0.5),
        "w_down_e": nrm(ks[16], (L, E, F, D), F ** -0.5),
        "w_sh_gate": nrm(ks[17], (L, D, SHARED_DIM), D ** -0.5),
        "w_sh_up": nrm(ks[18], (L, D, SHARED_DIM), D ** -0.5),
        "w_sh_down": nrm(ks[19], (L, SHARED_DIM, D), SHARED_DIM ** -0.5),
        "final_g": 1.0 + nrm(ks[20], (D,), 0.02),
    }

def reference(x, c, positions, ada_w, ada_b, norm1_g, w_in, attn_sinks, pool_w, pool_scale,
              w_out, norm2_g, w_router, router_bias, w_gate_e, w_up_e, w_down_e,
              w_sh_gate, w_sh_up, w_sh_down, final_g):
    for l in range(DEPTH):
        x = hybrid_layer(x, c, positions, ada_w[l], ada_b[l], norm1_g[l], w_in[l], attn_sinks[l],
                         pool_w[l], pool_scale[l], w_out[l], norm2_g[l], w_router[l],
                         router_bias[l], w_gate_e[l], w_up_e[l], w_down_e[l],
                         w_sh_gate[l], w_sh_up[l], w_sh_down[l])
    return rmsnorm(x, final_g)


_drawn_inputs = setup_inputs


def setup_inputs(seed=0):
    import zlib

    import numpy as np

    out = dict(_drawn_inputs(seed))
    spreads = {}
    factors = {'norm1_g': 3.485, 'attn_sinks': 200.0, 'final_g': 26.835}
    for name, (base, spread) in spreads.items():
        noise = np.random.default_rng([zlib.crc32(name.encode()), seed]).standard_normal(out[name].shape)
        drawn = base * np.exp(spread * noise) if base else spread * noise
        out[name] = __import__('jax').numpy.asarray(drawn.astype(out[name].dtype))
    for name, factor in factors.items():
        out[name] = (out[name] * factor).astype(out[name].dtype)
    return out
```

```python
import concourse.bass as bass
from concourse import mybir
from contextlib import ExitStack
import numpy as np

P = 128
T = 2048
D = 1024
KD = D // P
NT = T // P
HD = 64
NH = 8
QW = NH * HD
KVW = 2 * HD
PW = 512
NPG = 4
POOL_WINDOWS = (2, 4, 8, 16)
IN = QW + 2 * KVW + PW
ROT = 16
E = 128
F = 256
TOPK = 8
NG = 8
GE = E // NG
TOPG = 4
ROUTED_SCALE = 2.5
EPS = 1e-6
PAD = T
EW = 6144
SLOTS = 4
UNROLL = 8
AHEAD = 4
ACT_PER_TILE = 7
DVE_PER_TILE = 46
TAB = 3 * P
NEG = -1e30

COLS = dict(ident=P, band0=NPG * P, band=NPG * P, bandp=NPG * P, tri=P, cum=P, iota=P, base=P,
            blk=3, k128=16, ebase=1, inv=ROT, iotag=NG, tok=NT)
AT = {}
_n = 0
for _k, _w in COLS.items():
    AT[_k] = (_n, _w)
    _n += _w
NCONST = _n


def constants():
    c = np.zeros((P, NCONST), np.float32)

    def put(name, a):
        at, w = AT[name]
        c[:, at:at + w] = np.broadcast_to(a, (P, w))

    s, t = np.arange(P)[:, None], np.arange(P)[None, :]
    put("ident", np.eye(P))
    eye = np.eye(P)
    first, cur, prev = [], [], []
    for w in POOL_WINDOWS:
        inside = (t - s >= 0) & (t - s < w)
        first.append(inside / np.minimum(t + 1, w) - eye)
        cur.append(inside / w - eye)
        prev.append((t - (s - P) < w) / w)
    put("band0", np.concatenate(first, 1))
    put("band", np.concatenate(cur, 1))
    put("bandp", np.concatenate(prev, 1))
    put("tri", s < t)
    put("cum", s <= t)
    put("iota", t)
    put("base", t * T)
    put("blk", np.maximum(s - 1 + P * np.arange(3)[None, :], 0))
    put("k128", P * np.arange(16)[None, :])
    put("ebase", s * T)
    inv = np.power(500000.0, -np.arange(ROT // 2) * 2.0 / ROT).astype(np.float32)
    put("inv", np.concatenate([inv, inv])[None, :])
    put("iotag", np.arange(NG)[None, :])
    put("tok", s + P * np.arange(NT)[None, :])
    return c


class Chain:

    def __init__(self, eng, sem):
        self.eng, self.sem, self.base, self.n = eng, sem, 0, 0

    def link(self, ins):
        ins.then_inc(self.sem, 1)
        self.n += 1
        self.wait()

    def mark(self, ins):
        ins.then_inc(self.sem, 1)
        self.n += 1

    def wait(self):
        self.eng.wait_ge(self.sem, self.base + self.n)


def build(nc, A, out):
    f32, i32, u32, bf16 = mybir.dt.float32, mybir.dt.int32, mybir.dt.uint32, mybir.dt.bfloat16
    ALU, ACT, AX = mybir.AluOpType, mybir.ActivationFunctionType, mybir.AxisListType
    ctx = ExitStack()
    ctx.enter_context(nc.allow_non_contiguous_dma(reason="a few small vectors, columns of 4 bytes"))
    with ctx:
        def sb(name, shape, dt=f32):
            return ctx.enter_context(nc.sbuf_tensor(name, shape, dt))

        def sem(name):
            return ctx.enter_context(nc.semaphore(name))

        h2_tab = nc.dram_tensor("h2_tab", [T + P, D], f32).ap()
        x1_tab = nc.dram_tensor("x1_tab", [T, D], f32).ap()
        acc_tab = nc.dram_tensor("acc_tab", [T + P, D], f32).ap()
        rec_tab = nc.dram_tensor("rec_tab", [E * T, 2], i32).ap()
        row_tab = nc.dram_tensor("row_tab", [TAB], i32).ap()

        cst = sb("cst", [P, NCONST])

        def C(name):
            at, w = AT[name]
            return cst[:, at:at + w]

        ident = C("ident")
        W = sb("W", [P, 25600])
        w_in = W[:, 0:KD * IN].rearrange("p (k n) -> p k n", k=KD)
        w_out = W[:, 10240:18432].rearrange("p (k n) -> p k n", k=KD)
        w_sh = W[:, 18432:24576]
        w_rt = W[:, 24576:25600].rearrange("p (k n) -> p k n", k=KD)
        A1, B1, A2, B2, G1, G2 = (sb(n, [P, D]) for n in ("A1", "B1", "A2", "B2", "G1", "G2"))
        poolw = sb("poolw", [P, NPG, P])
        pscale = sb("pscale", [P, NPG])
        sinkb = sb("sinkb", [P, NH])
        rbias = sb("rbias", [P, E])
        trig = sb("trig", [P, 2, NT, ROT])
        c16 = sb("c16", [P, 3, P], bf16)
        tri16, ones16, mask16 = c16[:, 0, :], c16[:, 1, :], c16[:, 2, :]

        S = sb("S", [P, 17280])
        cut = [0]

        def take(*shape):
            n = int(np.prod(shape))
            a = S[:, cut[0]:cut[0] + n]
            cut[0] += n
            if len(shape) == 2:
                a = a.rearrange("p (a b) -> p a b", a=shape[0])
            return a

        xin = take(D)
        xn = take(D)
        xT = take(KD, P)
        xres = take(D)
        x1 = xres
        h2 = take(D)
        h2T = take(KD, P)
        qkf = take((NH + 2) * HD)
        qk = qkf.rearrange("p (a b) -> p a b", b=HD)
        vC = take(KVW)
        vE = take(KVW)
        uC = take(PW)
        uP = take(PW)
        qT = take(4, P)
        kb = take(2 * P)
        sc = take(NH, P)
        PT = take(NH, P)
        mx = take(NPG, P)
        mixT = take(KD, P)
        hs = take(F)
        hsT = take(2, P)
        accs = take(D)
        sq = take(D // 2).bitcast(bf16)
        oh = take(TOPK * P // 2).bitcast(bf16).rearrange("p (a b) -> p a b", a=TOPK)
        tmp = take(TOPK, P)
        tmpf = tmp.rearrange("p a b -> p (a b)")
        ropeA = take(NH + 2, ROT)
        ropeB = take(NH + 2, ROT)
        scores = take(E)
        choice = take(E)
        repl = take(E)
        base = take(E)
        rk = take(E)
        sg = take(F)
        small = take(64)
        assert cut[0] <= 17280, cut
        NSTRIP = 3
        ada = [W[:, 10240 + 4096 * n:10240 + 4096 * (n + 1)].rearrange("p (k n) -> p k n", k=KD) for n in range(NSTRIP)]
        adab = [W[:, 22528 + 512 * n:22528 + 512 * (n + 1)] for n in range(NSTRIP)]
        cb = S[:, 0:1024].rearrange("p (k n) -> p k n", k=KD)
        gains = S[:, 1024:3072].rearrange("p (a n) -> p a n", a=2)
        pad_rec = S[:, 3072:5120].bitcast(i32)
        zeros = S[:, 5120:6144]

        smallc = sb("smallc", [P, 256])
        col = lambda n, w=1: smallc[:, n:n + w]
        ssq1, v1, l1, y1, t1, r1 = (col(n) for n in range(6))
        ssq2, v2, l2, y2, t2, r2 = (col(n) for n in range(6, 12))
        smax, sden, sexp, sinv = (col(16 + 8 * n, 8) for n in range(4))
        m8g = col(48, 64)
        gs, gm8, gif, gm, gneg, m8, eif, s8 = (col(112 + 8 * n, 8) for n in range(8))
        wsum, winv = col(176), col(177)
        posf = col(184, 8)
        gsel = small[:, 0:NG * TOPG].rearrange("p (a b) -> p a b", a=NG)
        gi = sb("gi", [P, 8], u32)
        ei = sb("ei", [P, 8], u32)
        posi = sb("posi", [P, 8], i32)
        recs = sb("recs", [P, TOPK, 2])
        toki = sb("toki", [P, NT], i32)
        pos_i = sb("pos_i", [P, NT], i32)
        offi = sb("offi", [P, 3], i32)
        tab = S[0:1, 8192:8192 + TAB + E].bitcast(i32)
        thr = S[0:1, 8704:8704 + 2 * E]
        nblk_i = sb("nblk_i", [1, 1], i32)
        rec = sb("rec", [P, UNROLL, 2], i32)
        recf = rec[:, :, :].bitcast(f32)

        PB = ctx.enter_context(nc.psum_tensor("PB", [P, 8, 512], f32))
        B = [PB[:, n, :] for n in range(8)]

        names = """c_wt c_cst c_pos c_ada0 c_ada1 c_ada2 c_win c_small c_vec c_rest settled z_pool z_fill z_rec z_dve
            p_mod p_xT p_sc p_rk p_proj p_bd p_h2T p_PT p_rt p_gu p_pv p_py p_hsT p_qkT p_dn p_wo
            a_c a_trig a_xT a_exp a_qk a_u a_h2T a_PT a_rt a_eg a_v a_aT a_hsT a_qkT a_acc a_sq1 a_y1 a_sq2 a_y2 a_ch
            v_c v_cb v_mod v_trig v_wo v_x1 v_sub v_v1 v_v2 v_h2 v_P v_rank v_recs v_rope v_mx v_PT v_hs v_yT v_mask v_xn v_ch v_c16
            s_xin s_xres st_x1 st_h2 st_acc st_rec
            e_cnt e_nb e_cum e_off e_tab e_row e_thr
            w_d0 w_d1 w_d2 w_d3 w_loaded down_done rec_ld xg_r0 xg_r1 xg_r2 xg_r3 xg_used gu_done eg_done h_ready hT_tr hT_sb xgT_a xgT_v y_done y_a y_v added
            f_in0 f_in1 f_sum f_sq f_v f_ln f_y f_out f_st0 f_st1 f_g f_go f_ch""".split()
        s = {n: sem(n) for n in names}

        def W8(eng, name, val):
            if isinstance(val, int) and val <= 0:
                return
            eng.wait_ge(s[name], val)

        def settle(eng):
            eng.sem_inc(s["settled"], 1)

        def ok(j):
            return not isinstance(j, int) or 0 <= j < NT

        def tiles(eng, step, chain=None, per_tile=0):
            for i in range(-2, 2):
                step(i)
            if chain:
                n0 = chain.n
            with eng.Fori(2, 14) as i:
                if chain:
                    chain.base, chain.n = eng.snap(i * per_tile + (n0 - 2 * per_tile)), 0
                step(i)
                if chain:
                    assert chain.n == per_tile, ("per tile", chain.n)
            if chain:
                chain.base, chain.n = 0, n0 + 12 * per_tile
            for i in range(14, 18):
                step(i)

        def rows(table, i):
            return table[bass.ds(i * P, P), :]

        xg = [S[:, n * D:(n + 1) * D] for n in range(AHEAD)]
        xgT = S[:, 4096:5120].rearrange("p (k n) -> p k n", k=KD)
        ys = [S[:, 5120 + n * D:6144 + n * D] for n in range(2)]
        hb, hbT = S[:, 7168:7424], S[:, 7424:7680].rearrange("p (a b) -> p a b", a=2)
        eg = S[:, 7680:7936]

        fx, fa, fo = [xin, xn], [xres, tmpf], [h2, accs]
        fcols = [(ssq1, v1, l1, y1, t1, r1), (ssq2, v2, l2, y2, t2, r2)]

        block = ctx.enter_context(nc.Block())

        @block.sync
        def _(sp):
            sp.dma_start(cst[:, :], A["consts"]).then_inc(s["c_cst"], 16)
            sp.dma_start(smallc[:, 0:KD], A["c"][0, :].rearrange("(k p) -> p k", p=P)).then_inc(s["c_vec"], 16)
            sp.dma_start(sinkb[:, :], A["attn_sinks"][0:1, :].to_broadcast([P, NH])).then_inc(s["c_pos"], 16)
            sp.dma_start(pos_i[:, :], A["positions"][0, :].rearrange("(t p) -> p t", p=P)).then_inc(s["c_pos"], 16)
            ada_w = A["ada_w"][0].rearrange("(k p) n -> p k n", p=P)
            def strip(m):
                n = m % NSTRIP
                sp.dma_start(ada[n], ada_w[:, :, 512 * m:512 * (m + 1)]).then_inc(s[f"c_ada{n}"], 16)
                sp.dma_start(adab[n], A["ada_b"][0:1, 512 * m:512 * (m + 1)].to_broadcast([P, 512])).then_inc(s[f"c_ada{n}"], 16)

            for m in range(NSTRIP):
                strip(m)
            sp.dma_start(gains[:, 0, :], A["norm1_g"][0:1, :].to_broadcast([P, D])).then_inc(s["c_small"], 16)
            sp.dma_start(gains[:, 1, :], A["norm2_g"][0:1, :].to_broadcast([P, D])).then_inc(s["c_small"], 16)
            sp.wait_ge(s["z_rec"], 2)
            halves = rec_tab.rearrange("(e h t) a -> h e (t a)", e=E, h=2)
            for n in range(2):
                sp.dma_start(halves[n], pad_rec).then_inc(s["z_fill"], 16)
            sp.wait_ge(s["z_dve"], 1)
            sp.dma_start(h2_tab[T:T + P, :], zeros).then_inc(s["st_h2"], 16)
            for m in range(NSTRIP, 12):
                W8(sp, "v_mod", m - NSTRIP + 1)
                strip(m)
                if m == 5:
                    sp.dma_start(w_in, A["w_in"][0].rearrange("(k p) n -> p k n", p=P)).then_inc(s["c_win"], 16)
            sp.wait_ge(s["z_fill"], 32)
            sp.wait_ge(s["st_h2"], 16)
            sp.wait_ge(s["v_wo"], 1)
            sp.dma_start(xin, A["x"][0][0:P, :]).then_inc(s["s_xin"], 16)
            wo = A["w_out"][0]
            sp.dma_start(w_out[0:HD, 0:4, :], wo[0:256, :].rearrange("(j d) n -> d j n", d=HD)).then_inc(s["c_wt"], 16)
            sp.dma_start(w_out[HD:P, 0:4, :], wo[256:512, :].rearrange("(j d) n -> d j n", d=HD)).then_inc(s["c_wt"], 16)
            sp.dma_start(w_out[:, 4:8, :], wo[512:1024, :].rearrange("(j p) n -> p j n", p=P)).then_inc(s["c_wt"], 16)
            sp.dma_start(poolw[:, :, :], A["pool_w"][0].rearrange("g c d -> c g d")).then_inc(s["c_wt"], 16)
            sp.dma_start(pscale[:, :], A["pool_scale"][0, :].rearrange("(g d) -> d g", d=P)).then_inc(s["c_wt"], 16)
            gu = w_sh[:, 0:4096].rearrange("p (k a n) -> p k a n", k=KD, a=2)
            sp.dma_start(gu[:, :, 0, :], A["w_sh_gate"][0].rearrange("(k p) n -> p k n", p=P)).then_inc(s["c_rest"], 16)
            sp.dma_start(gu[:, :, 1, :], A["w_sh_up"][0].rearrange("(k p) n -> p k n", p=P)).then_inc(s["c_rest"], 16)
            sp.dma_start(w_sh[:, 4096:6144].rearrange("p (k n) -> p k n", k=2),
                         A["w_sh_down"][0].rearrange("(k p) n -> p k n", p=P)).then_inc(s["c_rest"], 16)
            sp.dma_start(w_rt, A["w_router"][0].rearrange("(k p) n -> p k n", p=P)).then_inc(s["c_rest"], 16)
            sp.dma_start(rbias[:, :], A["router_bias"][0:1, :].to_broadcast([P, E])).then_inc(s["c_rest"], 16)

            def step(i):
                if ok(i + 2) and not (isinstance(i, int) and i == -2):
                    W8(sp, "v_xn", i + 2)
                    sp.dma_start(xin, rows(A["x"][0], i + 2)).then_inc(s["s_xin"], 16)
                if ok(i - 1):
                    W8(sp, "v_x1", i)
                    sp.dma_start(rows(x1_tab, i - 1), x1).then_inc(s["st_x1"], 16)
                if ok(i - 1):
                    W8(sp, "v_h2", i)
                    sp.dma_start(rows(h2_tab, i - 1), h2).then_inc(s["st_h2"], 16)
                if ok(i):
                    W8(sp, "st_x1", 16 * i)
                    sp.dma_start(xres, rows(A["x"][0], i)).then_inc(s["s_xres"], 16)
                if ok(i - 1):
                    W8(sp, "a_acc", i)
                    sp.dma_start(rows(acc_tab, i - 1), accs).then_inc(s["st_acc"], 16)

            tiles(sp, step)

            sp.wait_ge(s["e_off"], 1)
            sp.dma_start(row_tab.rearrange("(a p) -> p a", p=P), offi[:, :]).then_inc(s["e_row"], 16)
            sp.wait_ge(s["e_row"], 16)
            sp.dma_start(tab[0:1, 0:TAB], row_tab.rearrange("(a n) -> a n", a=1)).then_inc(s["e_tab"], 16)
            sp.wait_ge(s["e_thr"], 1)

            def load_expert(e, slot):
                at = slot * EW
                guv = W[:, at:at + 4096].rearrange("p (k a n) -> p k a n", k=KD, a=2)
                sp.dma_start(guv[:, :, 0, :], A["w_gate_e"][0, e].rearrange("(k p) n -> p k n", p=P)).then_inc(s[f"w_d{slot}"], 16)
                sp.dma_start(guv[:, :, 1, :], A["w_up_e"][0, e].rearrange("(k p) n -> p k n", p=P)).then_inc(s[f"w_d{slot}"], 16)
                sp.dma_start(W[:, at + 4096:at + EW].rearrange("p (k n) -> p k n", k=2),
                             A["w_down_e"][0, e].rearrange("(k p) n -> p k n", p=P)).then_inc(s[f"w_d{slot}"], 16)

            def dyn(name, e):
                return A[name][0, bass.ds(e, 1)].rearrange("a (k p) n -> p (a k) n", p=P)

            def load_dyn(e, slot):
                at = slot * EW
                guv = W[:, at:at + 4096].rearrange("p (k a n) -> p k a n", k=KD, a=2)
                sp.dma_start(guv[:, :, 0, :], dyn("w_gate_e", e)).then_inc(s[f"w_d{slot}"], 16)
                sp.dma_start(guv[:, :, 1, :], dyn("w_up_e", e)).then_inc(s[f"w_d{slot}"], 16)
                sp.dma_start(W[:, at + 4096:at + EW].rearrange("p (k n) -> p k n", k=2),
                             dyn("w_down_e", e)).then_inc(s[f"w_d{slot}"], 16)

            sp.wait_ge(s["p_dn"], NT)
            for e in range(SLOTS):
                load_expert(e, e)
                if e:
                    sp.wait_ge(s[f"w_d{e - 1}"], 48)
                    sp.sem_inc(s["w_loaded"], 1)
            with sp.Fori(1, E // SLOTS) as q:
                for n in range(SLOTS):
                    need = sp.value_load(tab[0:1, bass.ds(q * SLOTS + (TAB + n - SLOTS), 1)], min_val=1, max_val=512)
                    sp.wait_ge(s["y_v"], need)
                    load_dyn(q * SLOTS + n, n)
                    if n:
                        sp.wait_ge(s[f"w_d{n - 1}"], 48 * q + 48)
                    else:
                        sp.wait_ge(s[f"w_d{SLOTS - 1}"], 48 * q)
                    sp.sem_inc(s["w_loaded"], 1)
            sp.wait_ge(s[f"w_d{SLOTS - 1}"], 48 * (E // SLOTS))
            sp.sem_inc(s["w_loaded"], 1)

            sp.dma_start(B2[:, :], A["final_g"].rearrange("(a n) -> a n", a=1).to_broadcast([P, D])).then_inc(s["f_g"], 16)
            sp.wait_ge(s["f_go"], 1)

            def f_load(t, n):
                sp.dma_start(fx[n], rows(x1_tab, t)).then_inc(s[f"f_in{n}"], 16)
                sp.dma_start(fa[n], rows(acc_tab, t)).then_inc(s[f"f_in{n}"], 16)

            def pair(q, more):
                for n in range(2):
                    if more:
                        sp.wait_ge(s["f_sum"], q * 2 + n + 1)
                        f_load(q * 2 + n + 2, n)
                for n in range(2):
                    sp.wait_ge(s["f_out"], q * 2 + n + 1)
                    sp.dma_start(rows(out, q * 2 + n), fo[n]).then_inc(s[f"f_st{n}"], 16)

            f_load(0, 0)
            f_load(1, 1)
            pair(0, True)
            with sp.Fori(1, NT // 2 - 1) as q:
                pair(q, True)
            pair(NT // 2 - 1, False)
            sp.wait_ge(s["f_st0"], 16 * (NT // 2))
            sp.wait_ge(s["f_st1"], 16 * (NT // 2))

        @block.gpsimd
        def _(g):
            v = pad_rec.rearrange("p (a b c) -> p a b c", b=P, c=2)
            g.iota(v[:, :, :, 0], pattern=[[0, T // P // 2], [1, P]], base=PAD, channel_multiplier=0).then_inc(s["z_rec"], 1)
            g.memset(v[:, :, :, 1], 0).then_inc(s["z_rec"], 1)
            g.iota(rec[:, :, 0], pattern=[[0, UNROLL]], base=PAD, channel_multiplier=1).then_inc(s["z_pool"], 1)
            g.memset(rec[:, :, 1], 0).then_inc(s["z_pool"], 1)

            g.wait_ge(s["z_dve"], 1)
            for n in range(2):
                at = T + n * (P // 2)
                g.dma_start(acc_tab[at:at + P // 2, :], zeros[0:P // 2, :]).then_inc(s["added"], 16)

            def step(i):
                if ok(i - 2):
                    W8(g, "v_recs", i - 1)
                    settle(g)
                    for j in range(TOPK):
                        g.indirect_dma_start(rec_tab, bass.IndirectOffsetOnAxis(ap=posi[:, j:j + 1], axis=0),
                                             recs[:, j, :].bitcast(i32), None).then_inc(s["st_rec"], 16)

            g.wait_ge(s["z_fill"], 32)
            tiles(g, step)

            g.wait_ge(s["st_rec"], 16 * TOPK * NT)
            g.wait_ge(s["e_tab"], 16)
            g.wait_ge(s["z_pool"], 2)
            g.wait_ge(s["e_thr"], 1)
            g.wait_ge(s["st_h2"], 16 + 16 * NT)
            g.wait_ge(s["st_acc"], 16 * NT)
            nblk = g.value_load(nblk_i[0:1, 0:1], min_val=1, max_val=255)

            def load_rec(b, slot):
                off = g.value_load(tab[0:1, bass.ds(b + 1, 1)] if not isinstance(b, int) else tab[0:1, b + 1:b + 2],
                                   min_val=0, max_val=E * T - P)
                g.dma_start(rec[:, slot, :], rec_tab[bass.ds(off, P), :]).then_inc(s["rec_ld"], 16)

            def gather(n):
                settle(g)
                g.indirect_dma_start(xg[n % AHEAD], None, h2_tab,
                                     bass.IndirectOffsetOnAxis(ap=rec[:, n % UNROLL, 0:1], axis=0)).then_inc(s[f"xg_r{n % AHEAD}"], 16)

            for n in range(AHEAD + 2):
                load_rec(n, n)
            g.wait_ge(s["rec_ld"], 16 * (AHEAD + 2))
            for n in range(AHEAD):
                gather(n)
            with g.Fori(0, 256 // UNROLL) as q:
                for n in range(UNROLL):
                    b = g.snap(q * UNROLL + n)
                    with g.If(b < nblk + 1):
                        g.wait_ge(s["xg_used"], b + 1)
                        g.wait_ge(s["rec_ld"], b * 16 + 16 * (AHEAD + 2))
                        gather(n + AHEAD)
                        g.wait_ge(s["y_a"], b + 1)
                        g.wait_ge(s["y_v"], b + 2)
                        g.wait_ge(s["added"], b * 16 + 32)
                        settle(g)
                        g.indirect_dma_start(acc_tab, bass.IndirectOffsetOnAxis(ap=rec[:, (n - 1) % UNROLL, 0:1], axis=0),
                                             ys[(n - 1) % 2], None, compute_op=ALU.add).then_inc(s["added"], 16)
                        load_rec(b + (AHEAD + 2), (n + AHEAD + 2) % UNROLL)
            g.wait_ge(s["added"], nblk * 16 + 48)
            g.wait_ge(s["rec_ld"], nblk * 16 + 16 * (AHEAD + 3))
            g.sem_inc(s["f_go"], 1)

        @block.scalar
        def _(act):
            ch = Chain(act, s["a_ch"])
            A_ = nc.scalar.activation
            act.wait_ge(s["c_vec"], 16)
            A_(smallc[:, 8:16], smallc[:, 0:8], ACT.Exp, scale=-1.0).then_inc(s["a_c"], 1)
            act.wait_ge(s["v_trig"], 2)
            A_(trig[:, 0], trig[:, 0], ACT.Sin)
            A_(trig[:, 1], trig[:, 1], ACT.Sin).then_inc(s["a_trig"], 1)

            def step(i):
                if ok(i + 1):
                    W8(act, "p_xT", i + 2)
                    A_(xT[:, 0:4, :], B[2].rearrange("p (a b) -> p a b", a=4), ACT.Copy)
                    A_(xT[:, 4:8, :], B[3].rearrange("p (a b) -> p a b", a=4), ACT.Copy).then_inc(s["a_xT"], 1)
                if ok(i - 1):
                    W8(act, "v_x1", i)
                    ch.link(A_(sq, x1, ACT.Square, accum_out=ssq2))
                    act.sem_inc(s["a_sq2"], 1)
                    W8(act, "v_v2", i)
                    ch.link(A_(l2, v2, ACT.Ln))
                    A_(y2, l2, ACT.Exp, scale=-0.5).then_inc(s["a_y2"], 1)
                if ok(i):
                    W8(act, "v_sub", i + 1)
                    A_(sexp, sexp, ACT.Exp)
                    A_(sc, sc, ACT.Exp).then_inc(s["a_exp"], 1)
                if ok(i + 1):
                    W8(act, "p_proj", i + 2)
                    A_(qk[:, 0:8, :].rearrange("p (j g) d -> p g j d", g=2), B[4].rearrange("p (g j d) -> p g j d", g=2, j=4), ACT.Copy)
                    A_(qk[:, 8:10, :], B[5][:, 0:P].rearrange("p (a b) -> p a b", a=2), ACT.Copy).then_inc(s["a_qk"], 1)
                    if ok(i):
                        W8(act, "p_bd", i + 1)
                        ch.link(A_(uP, uC, ACT.Copy))
                    A_(uC[:, 0:256], B[5][:, 256:512], ACT.Copy)
                    A_(uC[:, 256:512], B[6][:, 0:256], ACT.Copy).then_inc(s["a_u"], 1)
                if ok(i - 1):
                    W8(act, "p_h2T", i)
                    A_(h2T[:, 0:4, :], B[2].rearrange("p (a b) -> p a b", a=4), ACT.Copy)
                    A_(h2T[:, 4:8, :], B[3].rearrange("p (a b) -> p a b", a=4), ACT.Copy).then_inc(s["a_h2T"], 1)
                if ok(i):
                    W8(act, "p_PT", i + 1)
                    A_(PT[:, 0:4, :], B[0].rearrange("p (a b) -> p a b", a=4), ACT.Copy).then_inc(s["a_PT"], 1)
                if ok(i - 1):
                    W8(act, "p_rt", i)
                    W8(act, "v_mask", i - 1)
                    A_(scores, B[6][:, 0:E], ACT.Exp, scale=-1.0).then_inc(s["a_rt"], 1)
                    W8(act, "p_gu", i)
                    A_(sg, B[7][:, 0:F], ACT.Exp, scale=-1.0).then_inc(s["a_eg"], 1)
                if ok(i):
                    W8(act, "p_pv", i + 1)
                    A_(mixT[:, 0:4, :], B[0].rearrange("p (a b) -> p a b", a=4), ACT.Copy).then_inc(s["a_aT"], 1)
                if ok(i + 1):
                    if ok(i):
                        ch.link(A_(vE[HD:P, :], vC[HD:P, :], ACT.Copy))
                    A_(vE[0:HD, :], B[5][0:HD, P:2 * P], ACT.Copy)
                    A_(vC, B[5][:, P:2 * P], ACT.Copy).then_inc(s["a_v"], 1)
                if ok(i - 1):
                    W8(act, "p_hsT", i)
                    A_(hsT, B[2][:, 0:F].rearrange("p (a b) -> p a b", a=2), ACT.Copy).then_inc(s["a_hsT"], 1)
                if ok(i + 1):
                    W8(act, "p_qkT", i + 2)
                    A_(qT, B[6].rearrange("p (a b) -> p a b", a=4), ACT.Copy)
                    if ok(i):
                        ch.link(A_(kb[:, HD:P], kb[:, 3 * HD:4 * HD], ACT.Copy))
                    A_(kb[:, P:2 * P], B[7][:, 0:P], ACT.Copy)
                    A_(kb[:, 0:HD], B[7][:, 0:HD], ACT.Copy).then_inc(s["a_qkT"], 1)
                if ok(i - 1):
                    W8(act, "p_dn", i)
                    W8(act, "st_acc", 16 * i - 16)
                    A_(accs[:, 0:512], B[2], ACT.Copy)
                    A_(accs[:, 512:1024], B[3], ACT.Copy).then_inc(s["a_acc"], 1)
                if ok(i + 2):
                    W8(act, "s_xin", 16 * i + 48)
                    ch.link(A_(sq, xin, ACT.Square, accum_out=ssq1))
                    act.sem_inc(s["a_sq1"], 1)
                    W8(act, "v_v1", i + 3)
                    ch.link(A_(l1, v1, ACT.Ln))
                    A_(y1, l1, ACT.Exp, scale=-0.5).then_inc(s["a_y1"], 1)

            act.wait_ge(s["v_wo"], 1)
            tiles(act, step, ch, ACT_PER_TILE)

            act.wait_ge(s["e_tab"], 16)
            act.wait_ge(s["e_thr"], 1)
            nblk = act.value_load(nblk_i[0:1, 0:1], min_val=1, max_val=255)

            def xg_half():
                A_(xgT[:, 0:4, :], B[2].rearrange("p (a b) -> p a b", a=4), ACT.Copy).then_inc(s["xgT_a"], 1)

            act.sem_inc(s["hT_sb"], 1)
            act.wait_ge(s["xg_used"], 1)
            xg_half()
            with act.Fori(0, 256 // UNROLL) as q:
                for n in range(UNROLL):
                    b = act.snap(q * UNROLL + n)
                    with act.If(b < nblk + 1):
                        act.wait_ge(s["gu_done"], b + 1)
                        A_(eg, B[7][:, 0:F], ACT.Silu).then_inc(s["eg_done"], 1)
                        act.wait_ge(s["xg_used"], b + 2)
                        xg_half()
                        act.wait_ge(s["y_done"], b + 1)
                        act.wait_ge(s["added"], b * 16 + 16)
                        A_(ys[(n - 1) % 2][:, 0:512], B[4], ACT.Copy, scale=recf[:, (n - 1) % UNROLL, 1:2]).then_inc(s["y_a"], 1)
                        act.wait_ge(s["hT_tr"], b + 1)
                        A_(hbT, B[6][:, 0:F].rearrange("p (a b) -> p a b", a=2), ACT.Copy).then_inc(s["hT_sb"], 1)

            act.wait_ge(s["f_go"], 1)

            def pair(q):
                for n in range(2):
                    ss, vv, ll, yy = fcols[n][:4]
                    act.wait_ge(s["f_sum"], q * 2 + n + 1)
                    A_(sq, fo[n], ACT.Square, accum_out=ss).then_inc(s["f_sq"], 1)
                    act.wait_ge(s["f_v"], q * 2 + n + 1)
                    A_(ll, vv, ACT.Ln).then_inc(s["f_ln"], 1)
                    act.wait_ge(s["f_ln"], q * 2 + n + 1)
                    A_(yy, ll, ACT.Exp, scale=-0.5).then_inc(s["f_y"], 1)

            with act.Fori(0, NT // 2) as q:
                pair(q)

        @block.vector
        def _(v):
            ch = Chain(v, s["v_ch"])
            V = nc.vector
            link = ch.link

            V.memset(zeros, 0.0).then_inc(s["z_dve"], 1)
            v.wait_ge(s["c_vec"], 16)
            v.wait_ge(s["a_c"], 1)
            link(V.tensor_scalar_add(smallc[:, 8:16], smallc[:, 8:16], 1.0))
            link(V.reciprocal(smallc[:, 8:16], smallc[:, 8:16]))
            link(V.tensor_tensor(smallc[:, 8:16], smallc[:, 8:16], smallc[:, 0:8], ALU.mult))
            V.tensor_copy(cb, smallc[:, 8:16].unsqueeze(2).to_broadcast([P, KD, P])).then_inc(s["v_cb"], 1)

            v.wait_ge(s["c_pos"], 32)
            v.wait_ge(s["c_cst"], 16)
            link(V.tensor_copy(col(192, NT), pos_i[:, :]))
            ang = trig[:, 1]
            link(V.tensor_tensor(trig[:, 1], col(192, NT).unsqueeze(2).to_broadcast([P, NT, ROT]),
                                 C("inv").unsqueeze(1).to_broadcast([P, NT, ROT]), ALU.mult))
            MAGIC = 12582912.0
            turns = trig[:, 0]
            link(V.tensor_scalar(turns, ang, float(1 / (2 * np.pi)), MAGIC, ALU.mult, ALU.add))
            link(V.tensor_scalar(turns, turns, -MAGIC, None, ALU.add))
            c1 = 6.28125
            c2 = float(np.float32(np.round((2 * np.pi - c1) * 2 ** 20) / 2 ** 20))
            c3 = float(np.float32(2 * np.pi - c1 - c2))
            for c in (c1, c2, c3):
                link(V.scalar_tensor_tensor(out=ang, in0=turns, scalar=-c, in1=ang, op0=ALU.mult, op1=ALU.add))
            link(V.tensor_scalar(turns, ang, float(np.pi / 2), -2 * float(np.pi), ALU.is_gt, ALU.mult))
            link(V.scalar_tensor_tensor(out=turns, in0=ang, scalar=float(np.pi / 2), in1=turns, op0=ALU.add, op1=ALU.add))
            LIM = 3.1415925
            V.tensor_scalar(turns, turns, LIM, -LIM, ALU.min, ALU.max).then_inc(s["v_trig"], 1)
            V.tensor_scalar(ang, ang, LIM, -LIM, ALU.min, ALU.max).then_inc(s["v_trig"], 1)
            V.tensor_copy(tri16, C("tri")).then_inc(s["v_c16"], 1)
            V.memset(ones16, 1.0).then_inc(s["v_c16"], 1)
            V.tensor_copy(toki[:, :], C("tok"))
            v.wait_ge(s["a_trig"], 1)
            link(V.tensor_scalar(trig[:, 1, :, 0:8], trig[:, 1, :, 0:8], -1.0, None, ALU.mult))

            dst = [B1, A1, G1, B2, A2, G2]
            for m in range(12):
                v.wait_ge(s["p_mod"], m + 1)
                v.wait_ge(s[f"c_ada{m % NSTRIP}"], 32 * (m // NSTRIP + 1))
                h = (m % 2) * 512
                V.tensor_tensor(dst[m // 2][:, h:h + 512], B[m % 2], adab[m % NSTRIP], ALU.add).then_inc(s["v_mod"], 1)
            v.wait_ge(s["c_small"], 32)
            v.wait_ge(s["v_mod"], 12)
            link(V.scalar_tensor_tensor(out=A1[:, :], in0=A1[:, :], scalar=1.0, in1=gains[:, 0, :], op0=ALU.add, op1=ALU.mult))
            link(V.scalar_tensor_tensor(out=A2[:, :], in0=A2[:, :], scalar=1.0, in1=gains[:, 1, :], op0=ALU.add, op1=ALU.mult))
            v.wait_ge(s["z_fill"], 32)
            v.wait_ge(s["st_h2"], 16)
            v.wait_ge(s["added"], 32)
            V.memset(uP, 0.0)
            V.memset(vE, 0.0)
            V.memset(kb, 0.0)
            link(V.tensor_copy(base, C("base")))
            v.sem_inc(s["v_wo"], 1)

            def rstd(ssq, vv, y, t, r, ready, got, n):
                W8(v, ready[0], n)
                V.tensor_scalar(vv, ssq, 1.0 / D, EPS, ALU.mult, ALU.add).then_inc(s[ready[1]], 1)
                W8(v, got, n if ready[0] != "f_y" else n + 1)
                W8(v, ready[1], n)
                link(V.tensor_tensor(t, y, y, ALU.mult))
                link(V.tensor_tensor(t, t, vv, ALU.mult))
                link(V.tensor_scalar(t, t, -0.5, 1.5, ALU.mult, ALU.add))
                link(V.tensor_tensor(r, t, y, ALU.mult))

            def silu_up(t, gate):
                link(V.tensor_scalar_add(t, t, 1.0))
                link(V.reciprocal(t, t))
                link(V.tensor_tensor(t, t, gate, ALU.mult))

            def step(i):
                if ok(i - 1):
                    W8(v, "p_wo", i)
                    W8(v, "s_xres", 16 * i)
                    V.tensor_tensor(tmpf[:, 0:512], B[4], G1[:, 0:512], ALU.mult)
                    link(V.tensor_tensor(tmpf[:, 512:1024], B[5], G1[:, 512:1024], ALU.mult))
                    V.tensor_tensor(x1, tmpf, xres, ALU.add).then_inc(s["v_x1"], 1)
                if ok(i):
                    W8(v, "p_sc", i + 1)
                    V.tensor_scalar(sc[:, 0:4, :], B[0].rearrange("p (a b) -> p a b", a=4), HD ** -0.5, None, ALU.mult)
                    link(V.tensor_scalar(sc[:, 4:8, :], B[1].rearrange("p (a b) -> p a b", a=4), HD ** -0.5, None, ALU.mult))
                    if isinstance(i, int) and i == 0:
                        link(V.memset(sc[0:HD, :, HD:P], NEG))
                    link(V.tensor_reduce(smax, sc, AX.X, ALU.max))
                    link(V.tensor_tensor(smax, smax, sinkb[:, :], ALU.max))
                    V.tensor_tensor(sexp, sinkb[:, :], smax, ALU.subtract)
                    V.tensor_tensor(sc, sc, smax.unsqueeze(2).to_broadcast([P, NH, P]), ALU.subtract).then_inc(s["v_sub"], 1)
                if ok(i - 1):
                    rstd(ssq2, v2, y2, t2, r2, ("a_sq2", "v_v2"), "a_y2", i)
                    W8(v, "v_x1", i)
                    W8(v, "st_h2", 16 * i)
                    W8(v, "p_h2T", i - 1)
                    link(V.scalar_tensor_tensor(out=h2, in0=x1, scalar=r2, in1=A2[:, :], op0=ALU.mult, op1=ALU.mult))
                    V.tensor_tensor(h2, h2, B2[:, :], ALU.add).then_inc(s["v_h2"], 1)
                if ok(i):
                    W8(v, "a_exp", i + 1)
                    link(V.tensor_reduce(sden, sc, AX.X, ALU.add))
                    link(V.tensor_tensor(sden, sden, sexp, ALU.add))
                    link(V.reciprocal(sinv, sden))
                    V.tensor_tensor(sc, sc, sinv.unsqueeze(2).to_broadcast([P, NH, P]), ALU.mult).then_inc(s["v_P"], 1)
                if ok(i - 2):
                    W8(v, "p_rk", i - 1)
                    link(V.tensor_tensor(rk, B[6][:, 0:E], base, ALU.add))
                    V.tensor_tensor(base, base, B[6][:, E:2 * E], ALU.add).then_inc(s["v_rank"], 1)
                    W8(v, "st_rec", 128 * (i - 2))
                    link(V.tensor_tensor(tmp, oh, rk.unsqueeze(1).to_broadcast([P, TOPK, E]), ALU.mult))
                    link(V.tensor_reduce(posf, tmp, AX.X, ALU.add))
                    V.tensor_copy(posi[:, :], posf)
                    V.tensor_copy(recs[:, :, 1], s8)
                    tk = toki[:, bass.ds(i - 2, 1)] if not isinstance(i, int) else toki[:, i - 2:i - 1]
                    V.tensor_copy(recs[:, :, 0].bitcast(i32), tk.to_broadcast([P, TOPK])).then_inc(s["v_recs"], 1)
                if ok(i + 1):
                    W8(v, "a_qk", i + 2)
                    W8(v, "a_trig", 1)
                    cosv = trig[:, 0, bass.ds(i + 1, 1), :] if not isinstance(i, int) else trig[:, 0, i + 1:i + 2, :]
                    sinv_ = trig[:, 1, bass.ds(i + 1, 1), :] if not isinstance(i, int) else trig[:, 1, i + 1:i + 2, :]
                    V.tensor_tensor(ropeA, qk[:, :, 0:ROT], cosv.to_broadcast([P, NH + 2, ROT]), ALU.mult)
                    V.tensor_tensor(ropeB[:, :, 0:8], qk[:, :, 8:16], sinv_[:, :, 0:8].to_broadcast([P, NH + 2, 8]), ALU.mult)
                    link(V.tensor_tensor(ropeB[:, :, 8:16], qk[:, :, 0:8], sinv_[:, :, 8:16].to_broadcast([P, NH + 2, 8]), ALU.mult))
                    V.tensor_tensor(qk[:, :, 0:ROT], ropeA, ropeB, ALU.add).then_inc(s["v_rope"], 1)
                if ok(i):
                    W8(v, "p_bd", i + 1)
                    V.tensor_copy(mx, B[7].rearrange("p (a b) -> p a b", a=4)).then_inc(s["v_mx"], 1)
                    W8(v, "p_PT", i + 1)
                    V.tensor_copy(PT[:, 4:8, :], B[1].rearrange("p (a b) -> p a b", a=4)).then_inc(s["v_PT"], 1)
                if ok(i - 1):
                    W8(v, "a_eg", i)
                    silu_up(sg, B[7][:, 0:F])
                    V.tensor_tensor(hs, sg, B[7][:, F:2 * F], ALU.mult).then_inc(s["v_hs"], 1)
                if ok(i):
                    W8(v, "p_py", i + 1)
                    W8(v, "c_wt", 80)
                    for g_ in range(NPG):
                        last = V.tensor_scalar(mixT[:, 4 + g_, :], B[1][:, g_ * P:(g_ + 1) * P], pscale[:, g_:g_ + 1], None, ALU.mult)
                    last.then_inc(s["v_yT"], 1)
                if ok(i - 1):
                    W8(v, "a_rt", i)
                    W8(v, "c_rest", 80)
                    link(V.tensor_scalar_add(scores, scores, 1.0))
                    link(V.reciprocal(scores, scores))
                    link(V.tensor_tensor(choice, scores, rbias[:, :], ALU.add))
                    settle(v)
                    for g_ in range(NG):
                        last = V.max(m8g[:, 8 * g_:8 * g_ + 8], choice[:, GE * g_:GE * (g_ + 1)])
                    link(last)
                    m3 = m8g.rearrange("p (g n) -> p g n", g=NG)
                    link(V.tensor_tensor(gs, m3[:, :, 0], m3[:, :, 1], ALU.add))
                    settle(v)
                    link(V.max(gm8, gs))
                    settle(v)
                    link(V.max_index(gi[:, :], gm8, gs))
                    link(V.tensor_copy(gif, gi[:, :]))
                    link(V.tensor_tensor(gsel, C("iotag").unsqueeze(2).to_broadcast([P, NG, TOPG]),
                                         gif[:, 0:TOPG].unsqueeze(1).to_broadcast([P, NG, TOPG]), ALU.is_equal))
                    link(V.tensor_reduce(gm, gsel, AX.X, ALU.max))
                    link(V.tensor_scalar(gneg, gm, -1.0, 1e30, ALU.add, ALU.mult))
                    cv = choice.rearrange("p (g n) -> p g n", g=NG)
                    link(V.tensor_tensor(cv, cv, gm.unsqueeze(2).to_broadcast([P, NG, GE]), ALU.mult))
                    link(V.tensor_tensor(cv, cv, gneg.unsqueeze(2).to_broadcast([P, NG, GE]), ALU.add))
                    settle(v)
                    link(V.max(m8, choice))
                    settle(v)
                    V.max_index(ei[:, :], m8, choice)
                    settle(v)
                    link(V.match_replace(repl, m8, choice, -3e38))
                    W8(v, "p_rk", i - 1)
                    V.tensor_tensor(mask16, choice, repl, ALU.not_equal).then_inc(s["v_c16"], 1)
                    link(V.tensor_copy(eif, ei[:, :]))
                    link(V.tensor_tensor(oh, C("iota").unsqueeze(1).to_broadcast([P, TOPK, E]),
                                         eif.unsqueeze(2).to_broadcast([P, TOPK, E]), ALU.is_equal))
                    link(V.tensor_tensor(tmp, oh, scores.unsqueeze(1).to_broadcast([P, TOPK, E]), ALU.mult))
                    link(V.tensor_reduce(s8, tmp, AX.X, ALU.add))
                    link(V.tensor_reduce(wsum, s8, AX.X, ALU.add))
                    link(V.reciprocal(winv, wsum))
                    link(V.tensor_scalar(s8, s8, winv, ROUTED_SCALE, ALU.mult, ALU.mult))
                    v.sem_inc(s["v_mask"], 1)
                if ok(i + 2):
                    rstd(ssq1, v1, y1, t1, r1, ("a_sq1", "v_v1"), "a_y1", i + 3)
                    W8(v, "p_xT", i + 2)
                    link(V.scalar_tensor_tensor(out=xn, in0=xin, scalar=r1, in1=A1[:, :], op0=ALU.mult, op1=ALU.mult))
                    V.tensor_tensor(xn, xn, B1[:, :], ALU.add).then_inc(s["v_xn"], 1)

            tiles(v, step, ch, DVE_PER_TILE)

            link(V.tensor_tensor(rk, base, C("base"), ALU.subtract))
            v.sem_inc(s["e_cnt"], 1)
            v.wait_ge(s["e_nb"], 1)
            link(V.tensor_copy(wsum, B[6][:, 0:1]))
            link(V.tensor_tensor(small[:, 0:16], wsum.to_broadcast([P, 16]), C("k128"), ALU.is_gt))
            link(V.tensor_reduce(winv, small[:, 0:16], AX.X, ALU.add))
            link(V.tensor_copy(scores, winv.to_broadcast([P, E])))
            v.sem_inc(s["e_cnt"], 1)
            v.wait_ge(s["e_nb"], 2)
            link(V.tensor_copy(choice, B[6][:, P:2 * P]))
            V.tensor_copy(nblk_i[:, :], choice[0:1, E - 1:E])
            link(V.tensor_scalar(thr[0:1, 0:E], choice[0:1, :], 0.0, 1.0, ALU.is_gt, ALU.add))
            link(V.tensor_tensor(thr[0:1, E:2 * E], thr[0:1, 0:E], choice[0:1, :], ALU.add))
            link(V.tensor_copy(tab[0:1, TAB:TAB + E], thr[0:1, E:2 * E]))
            for n in range(3):
                b = C("blk")[:, n:n + 1]
                link(V.tensor_tensor(repl, choice, b.to_broadcast([P, E]), ALU.is_le))
                V.tensor_reduce(gs[:, n:n + 1], repl, AX.X, ALU.add)
                link(V.tensor_tensor(rk, repl, choice, ALU.mult))
                link(V.tensor_reduce(gm8[:, n:n + 1], rk, AX.X, ALU.max))
            link(V.tensor_tensor(gm[:, 0:3], C("blk"), gm8[:, 0:3], ALU.subtract))
            link(V.tensor_scalar(gm[:, 0:3], gm[:, 0:3], float(P), None, ALU.mult))
            link(V.scalar_tensor_tensor(out=gneg[:, 0:3], in0=gs[:, 0:3], scalar=float(T), in1=gm[:, 0:3], op0=ALU.mult, op1=ALU.add))
            link(V.tensor_scalar(gneg[:, 0:3], gneg[:, 0:3], float(E * T - P), None, ALU.min))
            V.tensor_copy(offi[:, :], gneg[:, 0:3]).then_inc(s["e_off"], 1)
            V.memset(hbT, 0.0).then_inc(s["y_v"], 1)
            v.wait_ge(s["y_v"], 1)
            v.sem_inc(s["e_thr"], 1)

            v.wait_ge(s["e_tab"], 16)
            nblk = v.value_load(nblk_i[0:1, 0:1], min_val=1, max_val=255)

            def xg_half():
                V.tensor_copy(xgT[:, 4:8, :], B[3].rearrange("p (a b) -> p a b", a=4)).then_inc(s["xgT_v"], 1)

            v.wait_ge(s["xg_used"], 1)
            xg_half()
            with v.Fori(0, 256 // UNROLL) as q:
                for n in range(UNROLL):
                    b = v.snap(q * UNROLL + n)
                    with v.If(b < nblk + 1):
                        v.wait_ge(s["eg_done"], b + 1)
                        V.tensor_tensor(hb, eg, B[7][:, F:2 * F], ALU.mult).then_inc(s["h_ready"], 1)
                        v.wait_ge(s["xg_used"], b + 2)
                        xg_half()
                        v.wait_ge(s["y_done"], b + 1)
                        v.wait_ge(s["added"], b * 16 + 16)
                        V.tensor_scalar(ys[(n - 1) % 2][:, 512:1024], B[5], recf[:, (n - 1) % UNROLL, 1:2], None, ALU.mult).then_inc(s["y_v"], 1)
            v.wait_ge(s["f_g"], 16)
            fch = Chain(v, s["f_ch"])

            def pair(q):
                for n in range(2):
                    t = q * 2 + n
                    ss, vv, ll, yy, tt, rr = fcols[n]
                    v.wait_ge(s[f"f_in{n}"], 32 * q + 32)
                    fch.link(V.tensor_tensor(fa[n], fa[n], G2[:, :], ALU.mult))
                    W8(v, f"f_st{n}", 16 * q)
                    V.tensor_tensor(fo[n], fa[n], fx[n], ALU.add).then_inc(s["f_sum"], 1)
                    v.wait_ge(s["f_sq"], t + 1)
                    V.tensor_scalar(vv, ss, 1.0 / D, EPS, ALU.mult, ALU.add).then_inc(s["f_v"], 1)
                for n in range(2):
                    t = q * 2 + n
                    ss, vv, ll, yy, tt, rr = fcols[n]
                    v.wait_ge(s["f_y"], t + 1)
                    v.wait_ge(s["f_v"], t + 1)
                    fch.link(V.tensor_tensor(tt, yy, yy, ALU.mult))
                    fch.link(V.tensor_tensor(tt, tt, vv, ALU.mult))
                    fch.link(V.tensor_scalar(tt, tt, -0.5, 1.5, ALU.mult, ALU.add))
                    fch.link(V.tensor_tensor(rr, tt, yy, ALU.mult))
                    v.wait_ge(s["f_sum"], t + 1)
                    V.scalar_tensor_tensor(out=fo[n], in0=fo[n], scalar=rr, in1=B2[:, :], op0=ALU.mult, op1=ALU.mult).then_inc(s["f_out"], 1)

            pair(0)
            per_pair = fch.n
            with v.Fori(1, NT // 2) as q:
                fch.base, fch.n = v.snap(q * per_pair), 0
                pair(q)

        @block.tensor
        def _(pe):
            mm, tr = nc.tensor.matmul, nc.tensor.transpose
            pe.wait_ge(s["v_cb"], 1)
            for m in range(12):
                pe.wait_ge(s[f"c_ada{m % NSTRIP}"], 32 * (m // NSTRIP + 1))
                W8(pe, "v_mod", m - 1)
                for k in range(KD):
                    last = mm(B[m % 2], cb[:, k, :], ada[m % NSTRIP][:, k, :], start=(k == 0), stop=(k == KD - 1))
                last.then_inc(s["p_mod"], 1)

            def transposes(banks, src, name):
                for k in range(KD):
                    last = tr(B[banks[k // 4]][:, (k % 4) * P:(k % 4 + 1) * P], src[:, k * P:(k + 1) * P], ident)
                last.then_inc(s[name], 1)

            def down(banks, lhsT, w, at, name):
                for n in range(2):
                    for k in range(2):
                        last = mm(B[banks[n]], lhsT[:, k, :], w(at + k * D + n * 512), start=(k == 0), stop=(k == 1))
                last.then_inc(s[name], 1)

            shw = lambda at: w_sh[:, at:at + 512]

            def step(i):
                if ok(i + 1):
                    W8(pe, "v_xn", i + 2)
                    W8(pe, "a_acc", i - 1)
                    transposes((2, 3), xn, "p_xT")
                if ok(i):
                    W8(pe, "a_qkT", i + 1)
                    settle(pe)
                    for h in range(NH):
                        g_, j = h // 4, h % 4
                        rs = slice(HD * g_, HD * g_ + HD)
                        for c in range(2):
                            last = mm(B[g_][c * HD:(c + 1) * HD, j * P:(j + 1) * P], qT[rs, j, c * HD:(c + 1) * HD],
                                      kb[rs, c * P:(c + 1) * P], start=True, stop=True)
                    last.then_inc(s["p_sc"], 1)
                if ok(i - 2):
                    W8(pe, "v_mask", i - 1)
                    W8(pe, "v_c16", i + 1)
                    W8(pe, "v_rank", i - 2)
                    mm(B[6][:, 0:E], tri16, mask16, start=True, stop=True)
                    mm(B[6][:, E:2 * E], ones16, mask16, start=True, stop=True).then_inc(s["p_rk"], 1)
                if ok(i + 1):
                    W8(pe, "a_xT", i + 2)
                    W8(pe, "v_x1", i)
                    for n, w in ((0, 512), (1, 512), (2, 256)):
                        if n == 2:
                            W8(pe, "v_rank", i - 1)
                        for k in range(KD):
                            last = mm(B[4 + n][:, 0:w], xT[:, k, :], w_in[:, k, n * 512:n * 512 + w], start=(k == 0), stop=(k == KD - 1))
                    last.then_inc(s["p_proj"], 1)
                if ok(i):
                    W8(pe, "a_u", i + 1)
                    bd = C("band0") if isinstance(i, int) and i == 0 else C("band")
                    for g_ in range(NPG):
                        cs = slice(g_ * P, (g_ + 1) * P)
                        mm(B[7][:, cs], uC[:, cs], bd[:, cs], start=True, stop=False)
                        last = mm(B[7][:, cs], uP[:, cs], C("bandp")[:, cs], start=False, stop=True)
                    last.then_inc(s["p_bd"], 1)
                if ok(i - 1):
                    W8(pe, "v_h2", i)
                    transposes((2, 3), h2, "p_h2T")
                if ok(i):
                    W8(pe, "v_P", i + 1)
                    for h in range(NH):
                        last = tr(B[h // 4][:, (h % 4) * P:(h % 4 + 1) * P], sc[:, h, :], ident)
                    last.then_inc(s["p_PT"], 1)
                if ok(i - 1):
                    W8(pe, "a_h2T", i)
                    W8(pe, "c_rest", 80)
                    if ok(i + 1):
                        W8(pe, "a_u", i + 2)
                    W8(pe, "v_rank", i - 1)
                    for k in range(KD):
                        last = mm(B[6][:, 0:E], h2T[:, k, :], w_rt[:, k, :], start=(k == 0), stop=(k == KD - 1))
                    last.then_inc(s["p_rt"], 1)
                    if ok(i):
                        W8(pe, "v_mx", i + 1)
                    for k in range(KD):
                        last = mm(B[7], h2T[:, k, :], shw(k * 512), start=(k == 0), stop=(k == KD - 1))
                    last.then_inc(s["p_gu"], 1)
                if ok(i):
                    W8(pe, "a_PT", i + 1)
                    W8(pe, "c_wt", 80)
                    W8(pe, "v_PT", i + 1)
                    W8(pe, "a_v", i + 1)
                    W8(pe, "v_mx", i + 1)
                    O = B[0].rearrange("p (a b) -> p a b", a=4)
                    for g_ in range(2):
                        for c, vv in ((0, vE), (1, vC)):
                            last = mm(O[g_ * HD:(g_ + 1) * HD, :, c * HD:(c + 1) * HD], vv[:, g_ * HD:(g_ + 1) * HD],
                                      PT[:, 4 * g_:4 * g_ + 4, c * HD:(c + 1) * HD], start=True, stop=True)
                    last.then_inc(s["p_pv"], 1)
                    for g_ in range(NPG):
                        last = mm(B[1][:, g_ * P:(g_ + 1) * P], poolw[:, g_, :], mx[:, g_, :], start=True, stop=True)
                    last.then_inc(s["p_py"], 1)
                if ok(i - 1):
                    W8(pe, "v_hs", i)
                    for k in range(2):
                        last = tr(B[2][:, k * P:(k + 1) * P], hs[:, k * P:(k + 1) * P], ident)
                    last.then_inc(s["p_hsT"], 1)
                if ok(i + 1):
                    W8(pe, "v_rope", i + 2)
                    W8(pe, "a_rt", i)
                    W8(pe, "a_u", i + 2)
                    for k in range(4):
                        tr(B[6][:, k * P:(k + 1) * P], qkf[:, k * P:(k + 1) * P], ident)
                    last = tr(B[7][:, 0:P], qkf[:, 4 * P:5 * P], ident)
                    last.then_inc(s["p_qkT"], 1)
                if ok(i - 1):
                    W8(pe, "a_hsT", i)
                    down((2, 3), hsT, shw, 4096, "p_dn")
                if ok(i):
                    W8(pe, "a_aT", i + 1)
                    W8(pe, "v_yT", i + 1)
                    if ok(i + 1):
                        W8(pe, "a_qk", i + 2)
                        W8(pe, "a_u", i + 2)
                        W8(pe, "a_v", i + 2)
                    for n in range(2):
                        for k in range(KD):
                            last = mm(B[4 + n], mixT[:, k, :], w_out[:, k, n * 512:(n + 1) * 512], start=(k == 0), stop=(k == KD - 1))
                    last.then_inc(s["p_wo"], 1)

            pe.wait_ge(s["v_wo"], 1)
            pe.wait_ge(s["c_win"], 16)
            tiles(pe, step)

            pe.wait_ge(s["e_cnt"], 1)
            tr(B[6][:, 0:P], rk, ident).then_inc(s["e_nb"], 1)
            pe.wait_ge(s["e_cnt"], 2)
            mm(B[6][:, P:2 * P], scores, C("cum"), start=True, stop=True).then_inc(s["e_nb"], 1)

            pe.wait_ge(s["e_tab"], 16)
            pe.wait_ge(s["e_thr"], 1)
            nblk = pe.value_load(nblk_i[0:1, 0:1], min_val=1, max_val=255)
            pe.wait_ge(s["a_acc"], NT)
            pe.wait_ge(s["xg_r0"], 16)
            transposes((2, 3), xg[0], "xg_used")
            with pe.Fori(0, 256 // UNROLL) as q:
                for n in range(UNROLL):
                    b = pe.snap(q * UNROLL + n)
                    with pe.If(b < nblk + 1):
                        off = pe.value_load(tab[0:1, bass.ds(b + 1, 1)], min_val=0, max_val=E * T - P)
                        before = pe.value_load(tab[0:1, bass.ds(b, 1)], min_val=0, max_val=E * T - P)
                        e = pe.snap(off // T)
                        at = pe.snap((e & (SLOTS - 1)) * EW)
                        pe.wait_ge(s["w_loaded"], e + 1)
                        pe.wait_ge(s["xgT_a"], b + 1)
                        pe.wait_ge(s["xgT_v"], b + 1)
                        for k in range(KD):
                            last = mm(B[7], xgT[:, k, :], W[:, bass.ds(at + k * 512, 512)], start=(k == 0), stop=(k == KD - 1))
                        last.then_inc(s["gu_done"], 1)
                        m = n + 1
                        pe.wait_ge(s[f"xg_r{m % AHEAD}"], (q * (UNROLL // AHEAD) + (m // AHEAD + 1)) * 16)
                        transposes((2, 3), xg[m % AHEAD], "xg_used")
                        pe.wait_ge(s["y_v"], b + 1)
                        pe.wait_ge(s["hT_sb"], b + 1)
                        at2 = pe.snap(((before // T) & (SLOTS - 1)) * EW)
                        down((4, 5), hbT, lambda x: W[:, bass.ds(at2 + x, 512)], 4096, "y_done")
                        pe.wait_ge(s["h_ready"], b + 1)
                        for k in range(2):
                            last = tr(B[6][:, k * P:(k + 1) * P], hb[:, k * P:(k + 1) * P], ident)
                        last.then_inc(s["hT_tr"], 1)


_INS = ["x", "c", "positions", "ada_w", "ada_b", "norm1_g", "w_in", "attn_sinks", "pool_w", "pool_scale", "w_out",
        "norm2_g", "w_router", "router_bias", "w_gate_e", "w_up_e", "w_down_e", "w_sh_gate", "w_sh_up", "w_sh_down",
        "final_g"]


def kernel(**inputs):
    import concourse.bacc as _bacc
    from concourse.bass_utils import run_bass_kernel_spmd as _run

    nc = _bacc.Bacc("TRN2", target_bir_lowering=False, num_devices=1)
    arrays, aps = {}, {}
    for name in _INS:
        arrays[f"in_{name}"] = np.ascontiguousarray(inputs[name])
    arrays["in_consts"] = constants()
    for name in _INS + ["consts"]:
        a = arrays[f"in_{name}"]
        aps[name] = nc.dram_tensor(f"in_{name}", a.shape, mybir.dt.from_np(a.dtype), kind="ExternalInput").ap()
    o = nc.dram_tensor("out_0", (T, D), mybir.dt.float32, kind="ExternalOutput").ap()
    build(nc, aps, o)
    r = _run(nc, [arrays], core_ids=[0])
    return r.results[0]["out_0"].reshape(1, T, D)
```

```python
import concourse.bass as bass
from concourse import mybir
from contextlib import ExitStack
import numpy as np

P = 128
T = 2048
D = 1024
KD = D // P
NT = T // P
HD = 64
NH = 8
QW = NH * HD
KVW = 2 * HD
PW = 512
NPG = 4
POOL_WINDOWS = (2, 4, 8, 16)
IN = QW + 2 * KVW + PW
ROT = 16
E = 128
F = 256
TOPK = 8
NG = 8
GE = E // NG
TOPG = 4
ROUTED_SCALE = 2.5
EPS = 1e-6
PAD = T
EW = 6144
SLOTS = 2
UNROLL = 8
AHEAD = 4
ACT_PER_TILE = 7
DVE_PER_TILE = 43
NTABS = 10
GUW = 4096
PIECE = 1024
NEG = -1e30

COLS = dict(ident=P, band0=NPG * P, band=NPG * P, bandp=NPG * P, tri=P, cum=P, iota=P, base=P,
            blk=3, after=3, start=3, second=3, shrec=2 * NT, k128=16, inv=ROT, iotag=NG, tok=NT)
AT = {}
_n = 0
for _k, _w in COLS.items():
    AT[_k] = (_n, _w)
    _n += _w
NCONST = _n


def constants():
    c = np.zeros((P, NCONST), np.float32)

    def put(name, a):
        at, w = AT[name]
        c[:, at:at + w] = np.broadcast_to(a, (P, w))

    s, t = np.arange(P)[:, None], np.arange(P)[None, :]
    put("ident", np.eye(P))
    eye = np.eye(P)
    first, cur, prev = [], [], []
    for w in POOL_WINDOWS:
        inside = (t - s >= 0) & (t - s < w)
        first.append(inside / np.minimum(t + 1, w) - eye)
        cur.append(inside / w - eye)
        prev.append((t - (s - P) < w) / w)
    put("band0", np.concatenate(first, 1))
    put("band", np.concatenate(cur, 1))
    put("bandp", np.concatenate(prev, 1))
    put("tri", s < t)
    put("cum", s <= t)
    put("iota", t)
    put("base", (t + 1) * T)
    put("blk", np.maximum(s - 1 + P * np.arange(3)[None, :], 0))
    put("after", c[:, AT["blk"][0]:AT["blk"][0] + 3] >= NT)
    put("second", c[:, AT["blk"][0]:AT["blk"][0] + 3] == 2)
    put("start", NT * c[:, AT["after"][0]:AT["after"][0] + 3])
    shrec = np.zeros((P, NT, 2), np.int32)
    shrec[:, :, 0] = NT * s + np.arange(NT)[None, :]
    shrec[:, :, 1] = np.float32(1.0).view(np.int32)
    put("shrec", shrec.reshape(P, 2 * NT).view(np.float32))
    put("k128", P * np.arange(16)[None, :])
    inv = np.power(500000.0, -np.arange(ROT // 2) * 2.0 / ROT).astype(np.float32)
    put("inv", np.concatenate([inv, inv])[None, :])
    put("iotag", np.arange(NG)[None, :])
    put("tok", s + P * np.arange(NT)[None, :])
    return c


class Chain:

    def __init__(self, eng, sem):
        self.eng, self.sem, self.base, self.n = eng, sem, 0, 0

    def link(self, ins):
        ins.then_inc(self.sem, 1)
        self.n += 1
        self.wait()

    def mark(self, ins):
        ins.then_inc(self.sem, 1)
        self.n += 1

    def wait(self):
        self.eng.wait_ge(self.sem, self.base + self.n)


def build(nc, A, out):
    f32, i32, u32, bf16 = mybir.dt.float32, mybir.dt.int32, mybir.dt.uint32, mybir.dt.bfloat16
    ALU, ACT, AX = mybir.AluOpType, mybir.ActivationFunctionType, mybir.AxisListType
    ctx = ExitStack()
    ctx.enter_context(nc.allow_non_contiguous_dma(reason="a few small vectors, columns of 4 bytes"))
    with ctx:
        def sb(name, shape, dt=f32):
            return ctx.enter_context(nc.sbuf_tensor(name, shape, dt))

        def sem(name):
            return ctx.enter_context(nc.semaphore(name))

        h2_tab = nc.dram_tensor("h2_tab", [T + P, D], f32).ap()
        acc_tab = nc.dram_tensor("acc_tab", [T + P, D], f32).ap()
        rec_tab = nc.dram_tensor("rec_tab", [(E + 1) * T, 2], i32).ap()
        row_tab = nc.dram_tensor("row_tab", [NTABS * P], i32).ap()

        cst = sb("cst", [P, NCONST])

        def C(name):
            at, w = AT[name]
            return cst[:, at:at + w]

        ident = C("ident")
        f32r = mybir.dt.float32r
        arena = sb("arena", [P, 48000])
        arena_at = nc.sbuf_base - 4 * 48000
        W = arena[:, 0:25600]
        w_in = W[:, 0:KD * IN].rearrange("p (k n) -> p k n", k=KD)
        w_out = W[:, 10240:18432].rearrange("p (k n) -> p k n", k=KD)
        w_rt = W[:, 24576:25600].rearrange("p (k n) -> p k n", k=KD)
        A1, B1, A2, B2, G1 = (arena[:, 42880 + n * D:42880 + (n + 1) * D] for n in range(5))
        G2 = sb("G2", [P, D])
        poolw = sb("poolw", [P, NPG, P])
        pscale = sb("pscale", [P, NPG])
        sinkb = sb("sinkb", [P, NH])
        rbias = sb("rbias", [P, E])
        trig = sb("trig", [P, 2, NT, ROT])
        c16 = sb("c16", [P, 3, P], bf16)
        tri16, ones16, mask16 = c16[:, 0, :], c16[:, 1, :], c16[:, 2, :]

        S = arena[:, 25600:42880]
        cut = [0]

        def take(*shape):
            n = int(np.prod(shape))
            a = S[:, cut[0]:cut[0] + n]
            cut[0] += n
            if len(shape) == 2:
                a = a.rearrange("p (a b) -> p a b", a=shape[0])
            return a

        xin = take(D)
        xn = take(D)
        xT = take(KD, P)
        xres = take(D)
        x1 = xres
        h2 = take(D)
        h2T = take(KD, P)
        qkf = take((NH + 2) * HD)
        qk = qkf.rearrange("p (a b) -> p a b", b=HD)
        vC = take(KVW)
        vE = take(KVW)
        uC = take(PW)
        uP = take(PW)
        qT = take(4, P)
        kb = take(2 * P)
        sc = take(NH, P)
        PT = take(NH, P)
        mx = take(NPG, P)
        mixT = take(KD, P)
        sq = take(D // 2).bitcast(bf16)
        oh = take(TOPK * P // 2).bitcast(bf16).rearrange("p (a b) -> p a b", a=TOPK)
        tmp = take(TOPK, P)
        tmpf = tmp.rearrange("p a b -> p (a b)")
        ropeA = take(NH + 2, ROT)
        ropeB = take(NH + 2, ROT)
        scores = take(E)
        choice = take(E)
        repl = take(E)
        base = take(E)
        rk = take(E)
        sg = take(F)
        small = take(64)
        assert cut[0] <= 17280, cut
        NSTRIP = 3
        ada = [W[:, 10240 + 4096 * n:10240 + 4096 * (n + 1)].rearrange("p (k n) -> p k n", k=KD) for n in range(NSTRIP)]
        adab = [W[:, 22528 + 512 * n:22528 + 512 * (n + 1)] for n in range(NSTRIP)]
        cb = S[:, 0:1024].rearrange("p (k n) -> p k n", k=KD)
        gains = S[:, 1024:3072].rearrange("p (a n) -> p a n", a=2)
        pad_rec = S[:, 3072:5120].bitcast(i32)
        zeros = S[:, 5120:6144]

        smallc = sb("smallc", [P, 256])
        col = lambda n, w=1: smallc[:, n:n + w]
        ssq1, v1, l1, y1, t1, r1 = (col(n) for n in range(6))
        ssq2, v2, l2, y2, t2, r2 = (col(n) for n in range(6, 12))
        smax, sden, sexp, sinv = (col(16 + 8 * n, 8) for n in range(4))
        m8g = col(48, 64)
        gs, gm8, gif, gm, gneg, m8, eif, s8 = (col(112 + 8 * n, 8) for n in range(8))
        wsum, winv = col(176), col(177)
        posf = col(184, 8)
        gsel = small[:, 0:NG * TOPG].rearrange("p (a b) -> p a b", a=NG)
        gi = sb("gi", [P, 8], u32)
        ei = sb("ei", [P, 8], u32)
        posi = sb("posi", [P, 8], i32)
        recs = sb("recs", [P, TOPK, 2])
        toki = sb("toki", [P, NT], i32)
        pos_i = sb("pos_i", [P, NT], i32)
        offi = sb("offi", [P, NTABS], i32)
        tab = cst[0:1, AT["band0"][0]:AT["band0"][0] + (NTABS + 1) * P].bitcast(i32)
        nblk_i = sb("nblk_i", [1, 2], i32)
        rec = sb("rec", [P, UNROLL, 2], i32)
        recf = rec[:, :, :].bitcast(f32)

        PB = ctx.enter_context(nc.psum_tensor("PB", [P, 8, 512], f32))
        B = [PB[:, n, :] for n in range(8)]

        names = """c_wt c_cst c_pos c_ada0 c_ada1 c_ada2 c_win c_small c_vec c_rest settled z_pool z_fill z_rec z_dve
            p_mod p_xT p_sc p_rk p_proj p_bd p_h2T p_PT p_rt p_pv p_py p_qkT p_wo
            a_c a_trig a_xT a_exp a_qk a_u a_h2T a_PT a_rt a_v a_aT a_qkT a_sq1 a_y1 a_sq2 a_y2 a_ch
            v_cb v_mod v_trig v_wo v_x1 v_sub v_v1 v_v2 v_h2 v_P v_rank v_recs v_rope v_mx v_PT v_yT v_mask v_xn v_ch v_c16
            s_xin s_xres st_x1 st_h2 st_rec
            e_cnt e_nb e_off e_tab e_row e_thr
            w_gu w_dn a_hig a_hid v_spg v_spd rec_ld xg_r0 xg_r1 xg_r2 xg_r3 xg_used gu_done eg_done h_ready hT_a hT_sb xgT_a xgT_v y_done y_v added
            f_in0 f_in1 f_in2 f_in3 f_in4 f_sq f_v f_ln f_y f_out f_st f_g f_go f_ch""".split()
        s = {n: sem(n) for n in names}

        def W8(eng, name, val):
            if isinstance(val, int) and val <= 0:
                return
            eng.wait_ge(s[name], val)

        def settle(eng):
            eng.sem_inc(s["settled"], 1)

        def ok(j):
            return not isinstance(j, int) or 0 <= j < NT

        def tiles(eng, step, chain=None, per_tile=0):
            for i in range(-2, 2):
                step(i)
            if chain:
                n0 = chain.n
            with eng.Fori(2, 14) as i:
                if chain:
                    chain.base, chain.n = eng.snap(i * per_tile + (n0 - 2 * per_tile)), 0
                step(i)
                if chain:
                    assert chain.n == per_tile, ("per tile", chain.n)
            if chain:
                chain.base, chain.n = 0, n0 + 12 * per_tile
            for i in range(14, 18):
                step(i)

        def rows(table, i):
            return table[bass.ds(i * P, P), :]

        def over(name, width, at, dt=f32):
            return nc.alloc_sbuf_tensor_at(name, [P, width], dt, offset=arena_at + 4 * at)

        RAW = over("RAW", SLOTS * EW, 0)
        WS = over("WS", 2 * SLOTS * EW, SLOTS * EW, f32r)
        WSf = WS[:, :].bitcast(f32)
        xg = [arena[:, 36864 + n * D:36864 + (n + 1) * D] for n in range(AHEAD)]
        XR = over("XR", 2 * D, 40960, f32r)
        xh, xl = (XR[:, n * D:(n + 1) * D].rearrange("p (k n) -> p k n", k=KD) for n in range(2))
        xhf = XR[:, 0:D].bitcast(f32).rearrange("p (k n) -> p k n", k=KD)
        ys = [arena[:, 43008 + n * D:43008 + (n + 1) * D] for n in range(2)]
        HR = over("HR", 512, 45056, f32r)
        hh, hl = (HR[:, n * F:(n + 1) * F].rearrange("p (k n) -> p k n", k=2) for n in range(2))
        hhf = HR[:, 0:F].bitcast(f32).rearrange("p (k n) -> p k n", k=2)
        hb = arena[:, 45568:45824]
        eg = arena[:, 45824:46080]
        FG = arena[:, 46080:47104]
        fsq = arena[:, NT * D:NT * D + NT * D // 2].bitcast(bf16).rearrange("p (t n) -> p t n", t=NT)

        fa = over("fa", NT * D, 0)[:, :].rearrange("p (t n) -> p t n", t=NT)
        fss, fv, fl, fy, ft, fr = (col(NT * n, NT) for n in range(6))
        groups = ((0, 2), (2, 6), (6, 10), (10, 14), (14, 16))

        block = ctx.enter_context(nc.Block())

        @block.sync
        def _(sp):
            sp.dma_start(cst[:, :], A["consts"]).then_inc(s["c_cst"], 16)
            sp.dma_start(smallc[:, 0:KD], A["c"][0, :].rearrange("(k p) -> p k", p=P)).then_inc(s["c_vec"], 16)
            sp.dma_start(sinkb[:, :], A["attn_sinks"][0:1, :].to_broadcast([P, NH])).then_inc(s["c_pos"], 16)
            sp.dma_start(pos_i[:, :], A["positions"][0, :].rearrange("(t p) -> p t", p=P)).then_inc(s["c_pos"], 16)
            ada_w = A["ada_w"][0].rearrange("(k p) n -> p k n", p=P)
            def strip(m):
                n = m % NSTRIP
                sp.dma_start(ada[n], ada_w[:, :, 512 * m:512 * (m + 1)]).then_inc(s[f"c_ada{n}"], 16)
                sp.dma_start(adab[n], A["ada_b"][0:1, 512 * m:512 * (m + 1)].to_broadcast([P, 512])).then_inc(s[f"c_ada{n}"], 16)

            for m in range(NSTRIP):
                strip(m)
            sp.dma_start(gains[:, 0, :], A["norm1_g"][0:1, :].to_broadcast([P, D])).then_inc(s["c_small"], 16)
            sp.dma_start(gains[:, 1, :], A["norm2_g"][0:1, :].to_broadcast([P, D])).then_inc(s["c_small"], 16)
            sp.wait_ge(s["z_rec"], 2)
            halves = rec_tab[T:(E + 1) * T, :].rearrange("(e h t) a -> h e (t a)", e=E, h=2)
            for n in range(2):
                sp.dma_start(halves[n], pad_rec).then_inc(s["z_fill"], 16)
            sp.wait_ge(s["c_cst"], 16)
            sp.dma_start(rec_tab[0:T, :].rearrange("(p t) a -> p (t a)", p=P), C("shrec").bitcast(i32)).then_inc(s["z_fill"], 16)
            sp.wait_ge(s["z_dve"], 1)
            sp.dma_start(h2_tab[T:T + P, :], zeros).then_inc(s["st_h2"], 16)
            for m in range(NSTRIP, 12):
                W8(sp, "v_mod", m - NSTRIP + 1)
                strip(m)
                if m == 5:
                    sp.dma_start(w_in, A["w_in"][0].rearrange("(k p) n -> p k n", p=P)).then_inc(s["c_win"], 16)
            sp.wait_ge(s["z_fill"], 48)
            sp.wait_ge(s["st_h2"], 16)
            sp.wait_ge(s["v_wo"], 1)
            sp.dma_start(xin, A["x"][0][0:P, :]).then_inc(s["s_xin"], 16)
            wo = A["w_out"][0]
            sp.dma_start(w_out[0:HD, 0:4, :], wo[0:256, :].rearrange("(j d) n -> d j n", d=HD)).then_inc(s["c_wt"], 16)
            sp.dma_start(w_out[HD:P, 0:4, :], wo[256:512, :].rearrange("(j d) n -> d j n", d=HD)).then_inc(s["c_wt"], 16)
            sp.dma_start(w_out[:, 4:8, :], wo[512:1024, :].rearrange("(j p) n -> p j n", p=P)).then_inc(s["c_wt"], 16)
            sp.dma_start(poolw[:, :, :], A["pool_w"][0].rearrange("g c d -> c g d")).then_inc(s["c_wt"], 16)
            sp.dma_start(pscale[:, :], A["pool_scale"][0, :].rearrange("(g d) -> d g", d=P)).then_inc(s["c_wt"], 16)
            sp.dma_start(w_rt, A["w_router"][0].rearrange("(k p) n -> p k n", p=P)).then_inc(s["c_rest"], 16)
            sp.dma_start(rbias[:, :], A["router_bias"][0:1, :].to_broadcast([P, E])).then_inc(s["c_rest"], 16)

            def step(i):
                if ok(i + 2) and not (isinstance(i, int) and i == -2):
                    W8(sp, "v_xn", i + 2)
                    sp.dma_start(xin, rows(A["x"][0], i + 2)).then_inc(s["s_xin"], 16)
                if ok(i - 1):
                    W8(sp, "v_x1", i)
                    sp.dma_start(rows(acc_tab, i - 1), x1).then_inc(s["st_x1"], 16)
                if ok(i - 1):
                    W8(sp, "v_h2", i)
                    sp.dma_start(rows(h2_tab, i - 1), h2).then_inc(s["st_h2"], 16)
                if ok(i):
                    W8(sp, "st_x1", 16 * i)
                    sp.dma_start(xres, rows(A["x"][0], i)).then_inc(s["s_xres"], 16)

            tiles(sp, step)

            def load(m, slot, part):
                at = slot * EW
                if isinstance(m, int) and m == 0:
                    src = lambda name: A[{"gate": "w_sh_gate", "up": "w_sh_up", "down": "w_sh_down"}[name]][0].rearrange("(k p) n -> p k n", p=P)
                else:
                    e = sp.value_load(tab[0:1, bass.ds(m + (9 * P - 1), 1)] if not isinstance(m, int) else tab[0:1, 9 * P + m - 1:9 * P + m],
                                      min_val=0, max_val=E - 1)
                    src = lambda name: A[f"w_{name}_e"][0, bass.ds(e, 1)].rearrange("a (k p) n -> p (a k) n", p=P)
                if part == "gu":
                    guv = RAW[:, at:at + GUW].rearrange("p (k a n) -> p k a n", k=KD, a=2)
                    sp.dma_start(guv[:, :, 0, :], src("gate")).then_inc(s["w_gu"], 16)
                    sp.dma_start(guv[:, :, 1, :], src("up")).then_inc(s["w_gu"], 16)
                else:
                    sp.dma_start(RAW[:, at + GUW:at + EW].rearrange("p (k n) -> p k n", k=2),
                                 src("down")).then_inc(s["w_dn"], 16)

            sp.wait_ge(s["p_proj"], NT)
            load(0, 0, "gu")
            load(0, 0, "dn")
            sp.wait_ge(s["e_off"], 1)
            sp.dma_start(row_tab.rearrange("(a p) -> p a", p=P), offi[:, :]).then_inc(s["e_row"], 16)
            sp.wait_ge(s["e_row"], 16)
            sp.dma_start(tab[:, 0:NTABS * P], row_tab.rearrange("(a n) -> a n", a=1)).then_inc(s["e_tab"], 16)
            sp.wait_ge(s["e_tab"], 16)
            sp.wait_ge(s["p_wo"], NT)
            nload = sp.value_load(nblk_i[0:1, 1:2], min_val=TOPK + 1, max_val=E + 1)

            sp.wait_ge(s["w_gu"], 32)
            load(1, 1, "gu")
            sp.wait_ge(s["w_dn"], 16)
            load(1, 1, "dn")
            with sp.Fori(1, E // SLOTS + 1) as q:
                for n in range(SLOTS):
                    m = sp.snap(q * SLOTS + n)
                    with sp.If(m < nload):
                        sp.wait_ge(s["w_gu"], m * 32)
                        settle(sp)
                        sp.wait_ge(s["v_spg"], m - 1)
                        settle(sp)
                        load(m, n, "gu")
                        sp.wait_ge(s["w_dn"], m * 16)
                        settle(sp)
                        sp.wait_ge(s["v_spd"], m - 1)
                        settle(sp)
                        load(m, n, "dn")
            sp.wait_ge(s["w_gu"], nload * 32)
            settle(sp)
            sp.wait_ge(s["w_dn"], nload * 16)
            settle(sp)

            sp.dma_start(FG, A["final_g"].rearrange("(a n) -> a n", a=1).to_broadcast([P, D])).then_inc(s["f_g"], 16)
            sp.wait_ge(s["f_go"], 1)

            for n, (lo, hi) in enumerate(groups):
                sp.dma_start(fa[:, lo:hi, :], acc_tab[lo * P:hi * P, :].rearrange("(t p) n -> p t n", p=P)).then_inc(s[f"f_in{n}"], 16)
            for t in range(NT):
                sp.wait_ge(s["f_out"], t + 1)
                sp.dma_start(out[t * P:(t + 1) * P, :], fa[:, t, :]).then_inc(s["f_st"], 16)
            sp.wait_ge(s["f_st"], 16 * NT)

        @block.gpsimd
        def _(g):
            v = pad_rec.rearrange("p (a b c) -> p a b c", b=P, c=2)
            g.iota(v[:, :, :, 0], pattern=[[0, T // P // 2], [1, P]], base=PAD, channel_multiplier=0).then_inc(s["z_rec"], 1)
            g.memset(v[:, :, :, 1], 0).then_inc(s["z_rec"], 1)
            g.iota(rec[:, :, 0], pattern=[[0, UNROLL]], base=PAD, channel_multiplier=1).then_inc(s["z_pool"], 1)
            g.memset(rec[:, :, 1], 0).then_inc(s["z_pool"], 1)

            g.wait_ge(s["z_dve"], 1)
            for n in range(2):
                at = T + n * (P // 2)
                g.dma_start(acc_tab[at:at + P // 2, :], zeros[0:P // 2, :]).then_inc(s["added"], 16)

            def step(i):
                if ok(i - 2):
                    W8(g, "v_recs", i - 1)
                    settle(g)
                    for j in range(TOPK):
                        g.indirect_dma_start(rec_tab, bass.IndirectOffsetOnAxis(ap=posi[:, j:j + 1], axis=0),
                                             recs[:, j, :].bitcast(i32), None).then_inc(s["st_rec"], 16)

            g.wait_ge(s["z_fill"], 48)
            g.wait_ge(s["z_pool"], 2)
            for n in range(AHEAD + 2):
                g.dma_start(rec[:, n, :], rec_tab[n * P:(n + 1) * P, :]).then_inc(s["rec_ld"], 16)
            tiles(g, step)

            def gather(n):
                settle(g)
                g.indirect_dma_start(xg[n % AHEAD], None, h2_tab,
                                     bass.IndirectOffsetOnAxis(ap=rec[:, n % UNROLL, 0:1], axis=0)).then_inc(s[f"xg_r{n % AHEAD}"], 16)

            g.wait_ge(s["e_off"], 1)
            g.wait_ge(s["st_h2"], 16 + 16 * NT)
            g.wait_ge(s["rec_ld"], 16 * (AHEAD + 2))
            for n in range(AHEAD):
                gather(n)
            g.wait_ge(s["st_rec"], 16 * TOPK * NT)
            g.wait_ge(s["e_tab"], 16)
            g.wait_ge(s["e_thr"], 1)
            g.wait_ge(s["st_x1"], 16 * NT)
            nblk = g.value_load(nblk_i[0:1, 0:1], min_val=NT + 1, max_val=NT + 255)

            def load_rec(b, slot):
                off = g.value_load(tab[0:1, bass.ds(b + 1, 1)],
                                   min_val=0, max_val=(E + 1) * T - P)
                g.dma_start(rec[:, slot, :], rec_tab[bass.ds(off, P), :]).then_inc(s["rec_ld"], 16)

            with g.Fori(0, (256 + NT) // UNROLL) as q:
                with g.If(q * UNROLL < nblk + 1):
                    for n in range(UNROLL):
                        b = g.snap(q * UNROLL + n)
                        with g.If(b < nblk + 1):
                            g.wait_ge(s["xg_used"], b + 1)
                            g.wait_ge(s["rec_ld"], b * 16 + 16 * (AHEAD + 2))
                            gather(n + AHEAD)
                            g.wait_ge(s["y_v"], b + 2)
                            g.wait_ge(s["added"], b * 16 + 32)
                            settle(g)
                            g.indirect_dma_start(acc_tab, bass.IndirectOffsetOnAxis(ap=rec[:, (n - 1) % UNROLL, 0:1], axis=0),
                                                 ys[(n - 1) % 2], None, compute_op=ALU.add).then_inc(s["added"], 16)
                            load_rec(b + (AHEAD + 2), (n + AHEAD + 2) % UNROLL)
                    settle(g)
            g.wait_ge(s["added"], nblk * 16 + 48)
            g.wait_ge(s["rec_ld"], nblk * 16 + 16 * (AHEAD + 3))
            g.sem_inc(s["f_go"], 1)

        @block.scalar
        def _(act):
            ch = Chain(act, s["a_ch"])
            A_ = nc.scalar.activation
            act.wait_ge(s["c_vec"], 16)
            A_(smallc[:, 8:16], smallc[:, 0:8], ACT.Exp, scale=-1.0).then_inc(s["a_c"], 1)
            act.wait_ge(s["v_trig"], 2)
            A_(trig[:, 0], trig[:, 0], ACT.Sin)
            A_(trig[:, 1], trig[:, 1], ACT.Sin).then_inc(s["a_trig"], 1)

            def step(i):
                if ok(i + 1):
                    W8(act, "p_xT", i + 2)
                    A_(xT[:, 0:4, :], B[2].rearrange("p (a b) -> p a b", a=4), ACT.Copy)
                    A_(xT[:, 4:8, :], B[3].rearrange("p (a b) -> p a b", a=4), ACT.Copy).then_inc(s["a_xT"], 1)
                if ok(i - 1):
                    W8(act, "v_x1", i)
                    ch.link(A_(sq, x1, ACT.Square, accum_out=ssq2))
                    act.sem_inc(s["a_sq2"], 1)
                    W8(act, "v_v2", i)
                    ch.link(A_(l2, v2, ACT.Ln))
                    A_(y2, l2, ACT.Exp, scale=-0.5).then_inc(s["a_y2"], 1)
                if ok(i):
                    W8(act, "v_sub", i + 1)
                    A_(sexp, sexp, ACT.Exp)
                    A_(sc, sc, ACT.Exp).then_inc(s["a_exp"], 1)
                if ok(i + 1):
                    W8(act, "p_proj", i + 2)
                    A_(qk[:, 0:8, :].rearrange("p (j g) d -> p g j d", g=2), B[4].rearrange("p (g j d) -> p g j d", g=2, j=4), ACT.Copy)
                    A_(qk[:, 8:10, :], B[5][:, 0:P].rearrange("p (a b) -> p a b", a=2), ACT.Copy).then_inc(s["a_qk"], 1)
                    if ok(i):
                        W8(act, "p_bd", i + 1)
                        ch.link(A_(uP, uC, ACT.Copy))
                    A_(uC[:, 0:256], B[5][:, 256:512], ACT.Copy)
                    A_(uC[:, 256:512], B[6][:, 0:256], ACT.Copy).then_inc(s["a_u"], 1)
                if ok(i - 1):
                    W8(act, "p_h2T", i)
                    A_(h2T[:, 0:4, :], B[2].rearrange("p (a b) -> p a b", a=4), ACT.Copy)
                    A_(h2T[:, 4:8, :], B[3].rearrange("p (a b) -> p a b", a=4), ACT.Copy).then_inc(s["a_h2T"], 1)
                if ok(i):
                    W8(act, "p_PT", i + 1)
                    A_(PT[:, 0:4, :], B[0].rearrange("p (a b) -> p a b", a=4), ACT.Copy).then_inc(s["a_PT"], 1)
                if ok(i - 1):
                    W8(act, "p_rt", i)
                    W8(act, "v_mask", i - 1)
                    A_(scores, B[6][:, 0:E], ACT.Exp, scale=-1.0).then_inc(s["a_rt"], 1)
                if ok(i):
                    W8(act, "p_pv", i + 1)
                    A_(mixT[:, 0:4, :], B[0].rearrange("p (a b) -> p a b", a=4), ACT.Copy).then_inc(s["a_aT"], 1)
                if ok(i + 1):
                    if ok(i):
                        ch.link(A_(vE[HD:P, :], vC[HD:P, :], ACT.Copy))
                    A_(vE[0:HD, :], B[5][0:HD, P:2 * P], ACT.Copy)
                    A_(vC, B[5][:, P:2 * P], ACT.Copy).then_inc(s["a_v"], 1)
                if ok(i + 1):
                    W8(act, "p_qkT", i + 2)
                    A_(qT, B[6].rearrange("p (a b) -> p a b", a=4), ACT.Copy)
                    if ok(i):
                        ch.link(A_(kb[:, HD:P], kb[:, 3 * HD:4 * HD], ACT.Copy))
                    A_(kb[:, P:2 * P], B[7][:, 0:P], ACT.Copy)
                    A_(kb[:, 0:HD], B[7][:, 0:HD], ACT.Copy).then_inc(s["a_qkT"], 1)
                if ok(i + 2):
                    W8(act, "s_xin", 16 * i + 48)
                    ch.link(A_(sq, xin, ACT.Square, accum_out=ssq1))
                    act.sem_inc(s["a_sq1"], 1)
                    W8(act, "v_v1", i + 3)
                    ch.link(A_(l1, v1, ACT.Ln))
                    A_(y1, l1, ACT.Exp, scale=-0.5).then_inc(s["a_y1"], 1)

            act.wait_ge(s["v_wo"], 1)
            tiles(act, step, ch, ACT_PER_TILE)

            act.wait_ge(s["e_tab"], 16)
            act.wait_ge(s["e_thr"], 1)
            nblk = act.value_load(nblk_i[0:1, 0:1], min_val=NT + 1, max_val=NT + 255)

            def upper(m, pieces):
                for k in pieces:
                    if isinstance(m, int):
                        r0, w0 = (m & 1) * EW + k * PIECE, (m & 1) * (2 * EW) + k * PIECE
                        to, of = WS[:, w0:w0 + PIECE], RAW[:, r0:r0 + PIECE]
                    else:
                        r0, w0 = act.snap((m & 1) * EW + k * PIECE), act.snap((m & 1) * (2 * EW) + k * PIECE)
                        to, of = WS[:, bass.ds(w0, PIECE)], RAW[:, bass.ds(r0, PIECE)]
                    nc.scalar.copy(to, of).then_inc(s["a_hig" if k < 4 else "a_hid"], 1)

            def rows_upper():
                for n in range(2):
                    A_(xh[:, 4 * n:4 * n + 4, :], B[2 + n].rearrange("p (a b) -> p a b", a=4), ACT.Copy).then_inc(s["xgT_a"], 1)

            act.wait_ge(s["w_gu"], 32)
            upper(0, range(4))
            act.wait_ge(s["xg_used"], 1)
            rows_upper()
            act.wait_ge(s["w_dn"], 16)
            upper(0, range(4, 6))
            with act.Fori(0, (256 + NT) // UNROLL) as q:
                with act.If(q * UNROLL < nblk + 1):
                    for n in range(UNROLL):
                        b = act.snap(q * UNROLL + n)
                        with act.If(b < nblk + 1):
                            md = act.value_load(tab[0:1, bass.ds(b + (6 * P + 1), 1)], min_val=0, max_val=E)
                            mg = act.value_load(tab[0:1, bass.ds(b + (6 * P + 2), 1)], min_val=0, max_val=E)
                            act.wait_ge(s["gu_done"], b + 2)
                            A_(eg, B[7][:, 0:F], ACT.Silu).then_inc(s["eg_done"], 1)
                            act.wait_ge(s["xg_used"], b + 2)
                            rows_upper()
                            with act.If(mg > 0):
                                act.wait_ge(s["w_gu"], mg * 32 + 32)
                                settle(act)
                                upper(mg, range(4))
                            act.wait_ge(s["y_done"], b + 1)
                            A_(hh, B[6][:, 0:F].rearrange("p (a b) -> p a b", a=2), ACT.Copy).then_inc(s["hT_a"], 1)
                            with act.If(md > 0):
                                act.wait_ge(s["w_dn"], md * 16 + 16)
                                settle(act)
                                upper(md, range(4, 6))
                            settle(act)
                    settle(act)

            for n, (lo, hi) in enumerate(groups):
                act.wait_ge(s[f"f_in{n}"], 16)
                for t in range(lo, hi):
                    A_(fsq[:, t, :], fa[:, t, :], ACT.Square, accum_out=fss[:, t:t + 1]).then_inc(s["f_sq"], 1)
                act.wait_ge(s["f_v"], n + 1)
                A_(fl[:, lo:hi], fv[:, lo:hi], ACT.Ln).then_inc(s["f_ln"], 1)
                act.wait_ge(s["f_ln"], n + 1)
                A_(fy[:, lo:hi], fl[:, lo:hi], ACT.Exp, scale=-0.5).then_inc(s["f_y"], 1)

        @block.vector
        def _(v):
            ch = Chain(v, s["v_ch"])
            V = nc.vector
            link = ch.link

            V.memset(zeros, 0.0).then_inc(s["z_dve"], 1)
            v.wait_ge(s["c_vec"], 16)
            v.wait_ge(s["a_c"], 1)
            link(V.tensor_scalar_add(smallc[:, 8:16], smallc[:, 8:16], 1.0))
            link(V.reciprocal(smallc[:, 8:16], smallc[:, 8:16]))
            link(V.tensor_tensor(smallc[:, 8:16], smallc[:, 8:16], smallc[:, 0:8], ALU.mult))
            V.tensor_copy(cb, smallc[:, 8:16].unsqueeze(2).to_broadcast([P, KD, P])).then_inc(s["v_cb"], 1)

            v.wait_ge(s["c_pos"], 32)
            v.wait_ge(s["c_cst"], 16)
            link(V.tensor_copy(col(192, NT), pos_i[:, :]))
            ang = trig[:, 1]
            link(V.tensor_tensor(trig[:, 1], col(192, NT).unsqueeze(2).to_broadcast([P, NT, ROT]),
                                 C("inv").unsqueeze(1).to_broadcast([P, NT, ROT]), ALU.mult))
            MAGIC = 12582912.0
            turns = trig[:, 0]
            link(V.tensor_scalar(turns, ang, float(1 / (2 * np.pi)), MAGIC, ALU.mult, ALU.add))
            link(V.tensor_scalar(turns, turns, -MAGIC, None, ALU.add))
            c1 = 6.28125
            c2 = float(np.float32(np.round((2 * np.pi - c1) * 2 ** 20) / 2 ** 20))
            c3 = float(np.float32(2 * np.pi - c1 - c2))
            for c in (c1, c2, c3):
                link(V.scalar_tensor_tensor(out=ang, in0=turns, scalar=-c, in1=ang, op0=ALU.mult, op1=ALU.add))
            link(V.tensor_scalar(turns, ang, float(np.pi / 2), -2 * float(np.pi), ALU.is_gt, ALU.mult))
            link(V.scalar_tensor_tensor(out=turns, in0=ang, scalar=float(np.pi / 2), in1=turns, op0=ALU.add, op1=ALU.add))
            LIM = 3.1415925
            V.tensor_scalar(turns, turns, LIM, -LIM, ALU.min, ALU.max).then_inc(s["v_trig"], 1)
            V.tensor_scalar(ang, ang, LIM, -LIM, ALU.min, ALU.max).then_inc(s["v_trig"], 1)
            V.tensor_copy(tri16, C("tri")).then_inc(s["v_c16"], 1)
            V.memset(ones16, 1.0).then_inc(s["v_c16"], 1)
            V.tensor_copy(toki[:, :], C("tok"))
            v.wait_ge(s["a_trig"], 1)
            link(V.tensor_scalar(trig[:, 1, :, 0:8], trig[:, 1, :, 0:8], -1.0, None, ALU.mult))

            dst = [B1, A1, G1, B2, A2, G2]
            for m in range(12):
                v.wait_ge(s["p_mod"], m + 1)
                v.wait_ge(s[f"c_ada{m % NSTRIP}"], 32 * (m // NSTRIP + 1))
                h = (m % 2) * 512
                V.tensor_tensor(dst[m // 2][:, h:h + 512], B[m % 2], adab[m % NSTRIP], ALU.add).then_inc(s["v_mod"], 1)
            v.wait_ge(s["c_small"], 32)
            v.wait_ge(s["v_mod"], 12)
            link(V.scalar_tensor_tensor(out=A1, in0=A1, scalar=1.0, in1=gains[:, 0, :], op0=ALU.add, op1=ALU.mult))
            link(V.scalar_tensor_tensor(out=A2, in0=A2, scalar=1.0, in1=gains[:, 1, :], op0=ALU.add, op1=ALU.mult))
            v.wait_ge(s["z_fill"], 48)
            v.wait_ge(s["st_h2"], 16)
            v.wait_ge(s["added"], 32)
            V.memset(uP, 0.0)
            V.memset(vE, 0.0)
            V.memset(kb, 0.0)
            link(V.tensor_copy(base, C("base")))
            v.sem_inc(s["v_wo"], 1)

            def rstd(ssq, vv, y, t, r, ready, got, n):
                W8(v, ready[0], n)
                V.tensor_scalar(vv, ssq, 1.0 / D, EPS, ALU.mult, ALU.add).then_inc(s[ready[1]], 1)
                W8(v, got, n if ready[0] != "f_y" else n + 1)
                W8(v, ready[1], n)
                link(V.tensor_tensor(t, y, y, ALU.mult))
                link(V.tensor_tensor(t, t, vv, ALU.mult))
                link(V.tensor_scalar(t, t, -0.5, 1.5, ALU.mult, ALU.add))
                link(V.tensor_tensor(r, t, y, ALU.mult))

            def step(i):
                if ok(i - 1):
                    W8(v, "p_wo", i)
                    W8(v, "s_xres", 16 * i)
                    V.tensor_tensor(tmpf[:, 0:512], B[4], G1[:, 0:512], ALU.mult)
                    link(V.tensor_tensor(tmpf[:, 512:1024], B[5], G1[:, 512:1024], ALU.mult))
                    V.tensor_tensor(x1, tmpf, xres, ALU.add).then_inc(s["v_x1"], 1)
                if ok(i):
                    W8(v, "p_sc", i + 1)
                    V.tensor_scalar(sc[:, 0:4, :], B[0].rearrange("p (a b) -> p a b", a=4), HD ** -0.5, None, ALU.mult)
                    link(V.tensor_scalar(sc[:, 4:8, :], B[1].rearrange("p (a b) -> p a b", a=4), HD ** -0.5, None, ALU.mult))
                    if isinstance(i, int) and i == 0:
                        link(V.memset(sc[0:HD, :, HD:P], NEG))
                    link(V.tensor_reduce(smax, sc, AX.X, ALU.max))
                    link(V.tensor_tensor(smax, smax, sinkb[:, :], ALU.max))
                    V.tensor_tensor(sexp, sinkb[:, :], smax, ALU.subtract)
                    V.tensor_tensor(sc, sc, smax.unsqueeze(2).to_broadcast([P, NH, P]), ALU.subtract).then_inc(s["v_sub"], 1)
                if ok(i - 1):
                    rstd(ssq2, v2, y2, t2, r2, ("a_sq2", "v_v2"), "a_y2", i)
                    W8(v, "v_x1", i)
                    W8(v, "st_h2", 16 * i)
                    W8(v, "p_h2T", i - 1)
                    link(V.scalar_tensor_tensor(out=h2, in0=x1, scalar=r2, in1=A2, op0=ALU.mult, op1=ALU.mult))
                    V.tensor_tensor(h2, h2, B2, ALU.add).then_inc(s["v_h2"], 1)
                if ok(i):
                    W8(v, "a_exp", i + 1)
                    link(V.tensor_reduce(sden, sc, AX.X, ALU.add))
                    link(V.tensor_tensor(sden, sden, sexp, ALU.add))
                    link(V.reciprocal(sinv, sden))
                    V.tensor_tensor(sc, sc, sinv.unsqueeze(2).to_broadcast([P, NH, P]), ALU.mult).then_inc(s["v_P"], 1)
                if ok(i - 2):
                    W8(v, "p_rk", i - 1)
                    link(V.tensor_tensor(rk, B[6][:, 0:E], base, ALU.add))
                    V.tensor_tensor(base, base, B[6][:, E:2 * E], ALU.add).then_inc(s["v_rank"], 1)
                    W8(v, "st_rec", 128 * (i - 2))
                    link(V.tensor_tensor(tmp, oh, rk.unsqueeze(1).to_broadcast([P, TOPK, E]), ALU.mult))
                    link(V.tensor_reduce(posf, tmp, AX.X, ALU.add))
                    V.tensor_copy(posi[:, :], posf)
                    V.tensor_copy(recs[:, :, 1], s8)
                    tk = toki[:, bass.ds(i - 2, 1)] if not isinstance(i, int) else toki[:, i - 2:i - 1]
                    V.tensor_copy(recs[:, :, 0].bitcast(i32), tk.to_broadcast([P, TOPK])).then_inc(s["v_recs"], 1)
                if ok(i + 1):
                    W8(v, "a_qk", i + 2)
                    W8(v, "a_trig", 1)
                    cosv = trig[:, 0, bass.ds(i + 1, 1), :] if not isinstance(i, int) else trig[:, 0, i + 1:i + 2, :]
                    sinv_ = trig[:, 1, bass.ds(i + 1, 1), :] if not isinstance(i, int) else trig[:, 1, i + 1:i + 2, :]
                    V.tensor_tensor(ropeA, qk[:, :, 0:ROT], cosv.to_broadcast([P, NH + 2, ROT]), ALU.mult)
                    V.tensor_tensor(ropeB[:, :, 0:8], qk[:, :, 8:16], sinv_[:, :, 0:8].to_broadcast([P, NH + 2, 8]), ALU.mult)
                    link(V.tensor_tensor(ropeB[:, :, 8:16], qk[:, :, 0:8], sinv_[:, :, 8:16].to_broadcast([P, NH + 2, 8]), ALU.mult))
                    V.tensor_tensor(qk[:, :, 0:ROT], ropeA, ropeB, ALU.add).then_inc(s["v_rope"], 1)
                if ok(i):
                    W8(v, "p_bd", i + 1)
                    V.tensor_copy(mx, B[7].rearrange("p (a b) -> p a b", a=4)).then_inc(s["v_mx"], 1)
                    W8(v, "p_PT", i + 1)
                    V.tensor_copy(PT[:, 4:8, :], B[1].rearrange("p (a b) -> p a b", a=4)).then_inc(s["v_PT"], 1)
                if ok(i):
                    W8(v, "p_py", i + 1)
                    W8(v, "c_wt", 80)
                    for g_ in range(NPG):
                        last = V.tensor_scalar(mixT[:, 4 + g_, :], B[1][:, g_ * P:(g_ + 1) * P], pscale[:, g_:g_ + 1], None, ALU.mult)
                    last.then_inc(s["v_yT"], 1)
                if ok(i - 1):
                    W8(v, "a_rt", i)
                    W8(v, "c_rest", 32)
                    link(V.tensor_scalar_add(scores, scores, 1.0))
                    link(V.reciprocal(scores, scores))
                    link(V.tensor_tensor(choice, scores, rbias[:, :], ALU.add))
                    settle(v)
                    for g_ in range(NG):
                        last = V.max(m8g[:, 8 * g_:8 * g_ + 8], choice[:, GE * g_:GE * (g_ + 1)])
                    link(last)
                    m3 = m8g.rearrange("p (g n) -> p g n", g=NG)
                    link(V.tensor_tensor(gs, m3[:, :, 0], m3[:, :, 1], ALU.add))
                    settle(v)
                    link(V.max(gm8, gs))
                    settle(v)
                    link(V.max_index(gi[:, :], gm8, gs))
                    link(V.tensor_copy(gif, gi[:, :]))
                    link(V.tensor_tensor(gsel, C("iotag").unsqueeze(2).to_broadcast([P, NG, TOPG]),
                                         gif[:, 0:TOPG].unsqueeze(1).to_broadcast([P, NG, TOPG]), ALU.is_equal))
                    link(V.tensor_reduce(gm, gsel, AX.X, ALU.max))
                    link(V.tensor_scalar(gneg, gm, -1.0, 1e30, ALU.add, ALU.mult))
                    cv = choice.rearrange("p (g n) -> p g n", g=NG)
                    link(V.tensor_tensor(cv, cv, gm.unsqueeze(2).to_broadcast([P, NG, GE]), ALU.mult))
                    link(V.tensor_tensor(cv, cv, gneg.unsqueeze(2).to_broadcast([P, NG, GE]), ALU.add))
                    settle(v)
                    link(V.max(m8, choice))
                    settle(v)
                    V.max_index(ei[:, :], m8, choice)
                    settle(v)
                    link(V.match_replace(repl, m8, choice, -3e38))
                    W8(v, "p_rk", i - 1)
                    V.tensor_tensor(mask16, choice, repl, ALU.not_equal).then_inc(s["v_c16"], 1)
                    link(V.tensor_copy(eif, ei[:, :]))
                    link(V.tensor_tensor(oh, C("iota").unsqueeze(1).to_broadcast([P, TOPK, E]),
                                         eif.unsqueeze(2).to_broadcast([P, TOPK, E]), ALU.is_equal))
                    link(V.tensor_tensor(tmp, oh, scores.unsqueeze(1).to_broadcast([P, TOPK, E]), ALU.mult))
                    link(V.tensor_reduce(s8, tmp, AX.X, ALU.add))
                    link(V.tensor_reduce(wsum, s8, AX.X, ALU.add))
                    link(V.reciprocal(winv, wsum))
                    link(V.tensor_scalar(s8, s8, winv, ROUTED_SCALE, ALU.mult, ALU.mult))
                    v.sem_inc(s["v_mask"], 1)
                if ok(i + 2):
                    rstd(ssq1, v1, y1, t1, r1, ("a_sq1", "v_v1"), "a_y1", i + 3)
                    W8(v, "p_xT", i + 2)
                    link(V.scalar_tensor_tensor(out=xn, in0=xin, scalar=r1, in1=A1, op0=ALU.mult, op1=ALU.mult))
                    V.tensor_tensor(xn, xn, B1, ALU.add).then_inc(s["v_xn"], 1)

            tiles(v, step, ch, DVE_PER_TILE)

            link(V.tensor_tensor(rk, base, C("base"), ALU.subtract))
            v.sem_inc(s["e_cnt"], 1)
            v.wait_ge(s["e_nb"], 1)
            link(V.tensor_copy(wsum, B[6][:, 0:1]))
            link(V.tensor_tensor(small[:, 0:16], wsum.to_broadcast([P, 16]), C("k128"), ALU.is_gt))
            link(V.tensor_reduce(winv, small[:, 0:16], AX.X, ALU.add))
            link(V.tensor_copy(scores, winv.to_broadcast([P, E])))
            link(V.tensor_scalar(sg[:, 0:E], scores, 1.0, None, ALU.min))
            v.sem_inc(s["e_cnt"], 1)
            v.wait_ge(s["e_nb"], 2)
            cumb, cumn = choice, sg[:, 0:E]
            V.tensor_scalar(cumb, B[6][:, P:2 * P], float(NT), None, ALU.add)
            link(V.tensor_copy(cumn, B[6][:, 2 * P:3 * P]))
            V.tensor_copy(nblk_i[:, 0:1], cumb[0:1, E - 1:E])
            nl = gs[:, 5:6]
            link(V.tensor_scalar(nl, cumn[:, E - 1:E], 1.0, None, ALU.add))
            V.tensor_copy(nblk_i[:, 1:2], nl[0:1, :])
            for n in range(3):
                b = C("blk")[:, n:n + 1]
                link(V.tensor_tensor(repl, cumb, b.to_broadcast([P, E]), ALU.is_le))
                V.tensor_reduce(gs[:, n:n + 1], repl, AX.X, ALU.add)
                V.tensor_tensor(sg[:, E:2 * E], repl, cumn, ALU.mult)
                link(V.tensor_tensor(rk, repl, cumb, ALU.mult))
                V.tensor_reduce(m8[:, n:n + 1], sg[:, E:2 * E], AX.X, ALU.max)
                link(V.tensor_reduce(gm8[:, n:n + 1], rk, AX.X, ALU.max))
            V.tensor_tensor(gs[:, 0:3], gs[:, 0:3], C("after"), ALU.add)
            V.tensor_tensor(m8[:, 0:3], m8[:, 0:3], C("after"), ALU.add)
            link(V.tensor_tensor(gm8[:, 0:3], gm8[:, 0:3], C("start"), ALU.max))
            link(V.tensor_tensor(gm[:, 0:3], C("blk"), gm8[:, 0:3], ALU.subtract))
            V.tensor_scalar(s8[:, 0:3], gm[:, 0:3], 0.0, None, ALU.is_equal)
            link(V.tensor_scalar(gneg[:, 0:3], gm[:, 0:3], float(P), None, ALU.mult))
            link(V.scalar_tensor_tensor(out=gneg[:, 0:3], in0=gs[:, 0:3], scalar=float(T), in1=gneg[:, 0:3], op0=ALU.mult, op1=ALU.add))
            V.tensor_scalar(offi[:, 0:3], gneg[:, 0:3], float((E + 1) * T - P), None, ALU.min)
            link(V.tensor_scalar(eif[:, 0:3], m8[:, 0:3], 1.0, None, ALU.add))
            link(V.tensor_tensor(posf[:, 0:3], eif[:, 0:3], nl.to_broadcast([P, 3]), ALU.is_lt))
            link(V.tensor_tensor(s8[:, 0:3], s8[:, 0:3], C("after"), ALU.mult))
            link(V.tensor_tensor(s8[:, 0:3], s8[:, 0:3], C("second"), ALU.add))
            link(V.tensor_tensor(posf[:, 0:3], posf[:, 0:3], s8[:, 0:3], ALU.mult))
            V.tensor_tensor(offi[:, 6:9], posf[:, 0:3], eif[:, 0:3], ALU.mult)
            V.tensor_tensor(offi[:, 3:6], m8[:, 0:3], cumn[:, E - 1:E].to_broadcast([P, 3]), ALU.min)
            link(V.tensor_tensor(repl, cumn, C("tok")[:, 0:1].to_broadcast([P, E]), ALU.is_le))
            link(V.tensor_reduce(gs[:, 4:5], repl, AX.X, ALU.add))
            V.tensor_copy(offi[:, 9:10], gs[:, 4:5]).then_inc(s["e_off"], 1)
            V.memset(HR[:, :].bitcast(f32), 0.0).then_inc(s["hT_sb"], 1)
            v.wait_ge(s["hT_sb"], 1)
            v.sem_inc(s["y_v"], 1)
            v.sem_inc(s["e_thr"], 1)

            v.wait_ge(s["e_tab"], 16)
            nblk = v.value_load(nblk_i[0:1, 0:1], min_val=NT + 1, max_val=NT + 255)

            def lower(m, pieces, done=None):
                for k in pieces:
                    if isinstance(m, int):
                        r0, w0 = (m & 1) * EW + k * PIECE, (m & 1) * (2 * EW) + k * PIECE
                        hi, lo, raw = WSf[:, w0:w0 + PIECE], WS[:, w0 + EW:w0 + EW + PIECE], RAW[:, r0:r0 + PIECE]
                    else:
                        r0, w0 = v.snap((m & 1) * EW + k * PIECE), v.snap((m & 1) * (2 * EW) + k * PIECE)
                        hi, lo, raw = WSf[:, bass.ds(w0, PIECE)], WS[:, bass.ds(w0 + EW, PIECE)], RAW[:, bass.ds(r0, PIECE)]
                    if k < 4:
                        v.wait_ge(s["a_hig"], m * 4 + (k + 1))
                    else:
                        v.wait_ge(s["a_hid"], m * 2 + (k - 3))
                    last = V.tensor_tensor(lo, raw, hi, ALU.subtract)
                if done:
                    last.then_inc(s[done], 1)

            def rows_lower(count):
                for n in range(2):
                    v.wait_ge(s["xgT_a"], count * 2 + (n + 1))
                    V.tensor_tensor(xl[:, 4 * n:4 * n + 4, :], B[2 + n].rearrange("p (a b) -> p a b", a=4),
                                    xhf[:, 4 * n:4 * n + 4, :], ALU.subtract).then_inc(s["xgT_v"], 1)

            lower(0, range(4), "v_spg")
            rows_lower(0)
            lower(0, range(4, 6), "v_spd")
            with v.Fori(0, (256 + NT) // UNROLL) as q:
                with v.If(q * UNROLL < nblk + 1):
                    for n in range(UNROLL):
                        b = v.snap(q * UNROLL + n)
                        with v.If(b < nblk + 1):
                            md = v.value_load(tab[0:1, bass.ds(b + (6 * P + 1), 1)], min_val=0, max_val=E)
                            mg = v.value_load(tab[0:1, bass.ds(b + (6 * P + 2), 1)], min_val=0, max_val=E)
                            v.wait_ge(s["eg_done"], b + 1)
                            V.tensor_tensor(hb, eg, B[7][:, F:2 * F], ALU.mult).then_inc(s["h_ready"], 1)
                            v.wait_ge(s["xg_used"], b + 2)
                            rows_lower(b + 1)
                            with v.If(mg > 0):
                                lower(mg, range(4), "v_spg")
                            v.wait_ge(s["y_done"], b + 1)
                            v.wait_ge(s["added"], b * 16 + 16)
                            for c in range(2):
                                last = V.scalar_tensor_tensor(out=ys[(n - 1) % 2][:, c * 512:(c + 1) * 512], in0=B[4 + c], scalar=recf[:, (n - 1) % UNROLL, 1:2],
                                                              in1=G2[:, c * 512:(c + 1) * 512], op0=ALU.mult, op1=ALU.mult)
                            last.then_inc(s["y_v"], 1)
                            v.wait_ge(s["hT_a"], b + 1)
                            V.tensor_tensor(hl, B[6][:, 0:F].rearrange("p (a b) -> p a b", a=2), hhf, ALU.subtract).then_inc(s["hT_sb"], 1)
                            with v.If(md > 0):
                                lower(md, range(4, 6), "v_spd")
                            settle(v)
                    settle(v)
            v.wait_ge(s["f_g"], 16)
            fch = Chain(v, s["f_ch"])
            for n, (lo, hi) in enumerate(groups):
                vv, yy, tt, rr = (a[:, lo:hi] for a in (fv, fy, ft, fr))
                v.wait_ge(s["f_sq"], hi)
                V.tensor_scalar(vv, fss[:, lo:hi], 1.0 / D, EPS, ALU.mult, ALU.add).then_inc(s["f_v"], 1)
                v.wait_ge(s["f_y"], n + 1)
                v.wait_ge(s["f_v"], n + 1)
                fch.link(V.tensor_tensor(tt, yy, yy, ALU.mult))
                fch.link(V.tensor_tensor(tt, tt, vv, ALU.mult))
                fch.link(V.tensor_scalar(tt, tt, -0.5, 1.5, ALU.mult, ALU.add))
                fch.link(V.tensor_tensor(rr, tt, yy, ALU.mult))
                for t in range(lo, hi):
                    V.scalar_tensor_tensor(out=fa[:, t, :], in0=fa[:, t, :], scalar=fr[:, t:t + 1], in1=FG, op0=ALU.mult, op1=ALU.mult).then_inc(s["f_out"], 1)

        @block.tensor
        def _(pe):
            mm, tr = nc.tensor.matmul, nc.tensor.transpose
            pe.wait_ge(s["v_cb"], 1)
            for m in range(12):
                pe.wait_ge(s[f"c_ada{m % NSTRIP}"], 32 * (m // NSTRIP + 1))
                W8(pe, "v_mod", m - 1)
                for k in range(KD):
                    last = mm(B[m % 2], cb[:, k, :], ada[m % NSTRIP][:, k, :], start=(k == 0), stop=(k == KD - 1))
                last.then_inc(s["p_mod"], 1)

            def transposes(banks, src, name):
                for k in range(KD):
                    last = tr(B[banks[k // 4]][:, (k % 4) * P:(k % 4 + 1) * P], src[:, k * P:(k + 1) * P], ident)
                last.then_inc(s[name], 1)

            def step(i):
                if ok(i + 1):
                    W8(pe, "v_xn", i + 2)
                    transposes((2, 3), xn, "p_xT")
                if ok(i):
                    W8(pe, "a_qkT", i + 1)
                    settle(pe)
                    for h in range(NH):
                        g_, j = h // 4, h % 4
                        rs = slice(HD * g_, HD * g_ + HD)
                        for c in range(2):
                            last = mm(B[g_][c * HD:(c + 1) * HD, j * P:(j + 1) * P], qT[rs, j, c * HD:(c + 1) * HD],
                                      kb[rs, c * P:(c + 1) * P], start=True, stop=True)
                    last.then_inc(s["p_sc"], 1)
                if ok(i - 2):
                    W8(pe, "v_mask", i - 1)
                    W8(pe, "v_c16", i + 1)
                    W8(pe, "v_rank", i - 2)
                    mm(B[6][:, 0:E], tri16, mask16, start=True, stop=True)
                    mm(B[6][:, E:2 * E], ones16, mask16, start=True, stop=True).then_inc(s["p_rk"], 1)
                if ok(i + 1):
                    W8(pe, "a_xT", i + 2)
                    W8(pe, "v_x1", i)
                    for n, w in ((0, 512), (1, 512), (2, 256)):
                        if n == 2:
                            W8(pe, "v_rank", i - 1)
                        for k in range(KD):
                            last = mm(B[4 + n][:, 0:w], xT[:, k, :], w_in[:, k, n * 512:n * 512 + w], start=(k == 0), stop=(k == KD - 1))
                    last.then_inc(s["p_proj"], 1)
                if ok(i):
                    W8(pe, "a_u", i + 1)
                    bd = C("band0") if isinstance(i, int) and i == 0 else C("band")
                    for g_ in range(NPG):
                        cs = slice(g_ * P, (g_ + 1) * P)
                        mm(B[7][:, cs], uC[:, cs], bd[:, cs], start=True, stop=False)
                        last = mm(B[7][:, cs], uP[:, cs], C("bandp")[:, cs], start=False, stop=True)
                    last.then_inc(s["p_bd"], 1)
                if ok(i - 1):
                    W8(pe, "v_h2", i)
                    transposes((2, 3), h2, "p_h2T")
                if ok(i):
                    W8(pe, "v_P", i + 1)
                    for h in range(NH):
                        last = tr(B[h // 4][:, (h % 4) * P:(h % 4 + 1) * P], sc[:, h, :], ident)
                    last.then_inc(s["p_PT"], 1)
                if ok(i - 1):
                    W8(pe, "a_h2T", i)
                    W8(pe, "c_rest", 32)
                    if ok(i + 1):
                        W8(pe, "a_u", i + 2)
                    W8(pe, "v_rank", i - 1)
                    for k in range(KD):
                        last = mm(B[6][:, 0:E], h2T[:, k, :], w_rt[:, k, :], start=(k == 0), stop=(k == KD - 1))
                    last.then_inc(s["p_rt"], 1)
                if ok(i):
                    W8(pe, "a_PT", i + 1)
                    W8(pe, "c_wt", 80)
                    W8(pe, "v_PT", i + 1)
                    W8(pe, "a_v", i + 1)
                    W8(pe, "v_mx", i + 1)
                    O = B[0].rearrange("p (a b) -> p a b", a=4)
                    for g_ in range(2):
                        for c, vv in ((0, vE), (1, vC)):
                            last = mm(O[g_ * HD:(g_ + 1) * HD, :, c * HD:(c + 1) * HD], vv[:, g_ * HD:(g_ + 1) * HD],
                                      PT[:, 4 * g_:4 * g_ + 4, c * HD:(c + 1) * HD], start=True, stop=True)
                    last.then_inc(s["p_pv"], 1)
                    for g_ in range(NPG):
                        last = mm(B[1][:, g_ * P:(g_ + 1) * P], poolw[:, g_, :], mx[:, g_, :], start=True, stop=True)
                    last.then_inc(s["p_py"], 1)
                if ok(i + 1):
                    W8(pe, "v_rope", i + 2)
                    W8(pe, "a_rt", i)
                    W8(pe, "a_u", i + 2)
                    for k in range(4):
                        tr(B[6][:, k * P:(k + 1) * P], qkf[:, k * P:(k + 1) * P], ident)
                    last = tr(B[7][:, 0:P], qkf[:, 4 * P:5 * P], ident)
                    last.then_inc(s["p_qkT"], 1)
                if ok(i):
                    W8(pe, "a_aT", i + 1)
                    W8(pe, "v_yT", i + 1)
                    if ok(i + 1):
                        W8(pe, "a_qk", i + 2)
                        W8(pe, "a_u", i + 2)
                        W8(pe, "a_v", i + 2)
                    for n in range(2):
                        for k in range(KD):
                            last = mm(B[4 + n], mixT[:, k, :], w_out[:, k, n * 512:(n + 1) * 512], start=(k == 0), stop=(k == KD - 1))
                    last.then_inc(s["p_wo"], 1)

            pe.wait_ge(s["v_wo"], 1)
            pe.wait_ge(s["c_win"], 16)
            tiles(pe, step)

            pe.wait_ge(s["e_cnt"], 1)
            tr(B[6][:, 0:P], rk, ident).then_inc(s["e_nb"], 1)
            pe.wait_ge(s["e_cnt"], 2)
            mm(B[6][:, P:2 * P], scores, C("cum"), start=True, stop=True)
            mm(B[6][:, 2 * P:3 * P], sg[:, 0:E], C("cum"), start=True, stop=True).then_inc(s["e_nb"], 1)

            pe.wait_ge(s["e_tab"], 16)
            pe.wait_ge(s["e_thr"], 1)
            nblk = pe.value_load(nblk_i[0:1, 0:1], min_val=NT + 1, max_val=NT + 255)
            pe.sem_inc(s["gu_done"], 1)
            pe.wait_ge(s["xg_r0"], 16)
            transposes((2, 3), xg[0], "xg_used")

            def parts(bank, hi, lo, w, K):
                for k in range(K):
                    mm(bank, hi[:, k, :], w(k, 0), start=(k == 0), stop=False)
                    mm(bank, hi[:, k, :], w(k, EW), start=False, stop=False)
                    last = mm(bank, lo[:, k, :], w(k, 0), start=False, stop=(k == K - 1))
                return last

            with pe.Fori(0, (256 + NT) // UNROLL) as q:
                with pe.If(q * UNROLL < nblk + 1):
                    for n in range(UNROLL):
                        b = pe.snap(q * UNROLL + n)
                        with pe.If(b < nblk + 1):
                            l1 = pe.value_load(tab[0:1, bass.ds(b + (3 * P + 1), 1)], min_val=0, max_val=E)
                            at = pe.snap((l1 & 1) * (2 * EW))
                            pe.wait_ge(s["v_spg"], l1 + 1)
                            pe.wait_ge(s["xgT_a"], b * 2 + 2)
                            pe.wait_ge(s["xgT_v"], b * 2 + 2)
                            parts(B[7], xh, xl, lambda k, o: WS[:, bass.ds(at + (o + k * 512), 512)], KD).then_inc(s["gu_done"], 1)
                            m = n + 1
                            pe.wait_ge(s[f"xg_r{m % AHEAD}"], (q * (UNROLL // AHEAD) + (m // AHEAD + 1)) * 16)
                            transposes((2, 3), xg[m % AHEAD], "xg_used")
                            l0 = pe.value_load(tab[0:1, bass.ds(b + 3 * P, 1)], min_val=0, max_val=E)
                            pe.wait_ge(s["y_v"], b + 1)
                            pe.wait_ge(s["hT_sb"], b + 1)
                            pe.wait_ge(s["v_spd"], l0 + 1)
                            at0 = pe.snap((l0 & 1) * (2 * EW))
                            down_w = lambda c: lambda k, o: WS[:, bass.ds(at0 + (o + GUW + k * D + c * 512), 512)]
                            parts(B[4], hh, hl, down_w(0), 2)
                            pe.wait_ge(s["h_ready"], b + 1)
                            for k in range(2):
                                tr(B[6][:, k * P:(k + 1) * P], hb[:, k * P:(k + 1) * P], ident)
                            parts(B[5], hh, hl, down_w(1), 2).then_inc(s["y_done"], 1)
                    settle(pe)


_INS = ["x", "c", "positions", "ada_w", "ada_b", "norm1_g", "w_in", "attn_sinks", "pool_w", "pool_scale", "w_out",
        "norm2_g", "w_router", "router_bias", "w_gate_e", "w_up_e", "w_down_e", "w_sh_gate", "w_sh_up", "w_sh_down",
        "final_g"]


def kernel(**inputs):
    import concourse.bacc as _bacc
    from concourse.bass_utils import run_bass_kernel_spmd as _run

    nc = _bacc.Bacc("TRN2", target_bir_lowering=False, num_devices=1)
    arrays, aps = {}, {}
    for name in _INS:
        arrays[f"in_{name}"] = np.ascontiguousarray(inputs[name])
    arrays["in_consts"] = constants()
    for name in _INS + ["consts"]:
        a = arrays[f"in_{name}"]
        aps[name] = nc.dram_tensor(f"in_{name}", a.shape, mybir.dt.from_np(a.dtype), kind="ExternalInput").ap()
    o = nc.dram_tensor("out_0", (T, D), mybir.dt.float32, kind="ExternalOutput").ap()
    build(nc, aps, o)
    r = _run(nc, [arrays], core_ids=[0])
    return r.results[0]["out_0"].reshape(1, T, D)
```
